# Optimizing a Trainium2 kernel written in Bass

```python
import jax
import jax.numpy as jnp
from jax import lax
import numpy as np

D_MODEL = 2048
BATCH = 1
SEQ = 256
DEPTH = 2
DEC_BATCH = 1
DEC_SEQ = 32
PAST_LEN = 512

CHUNK = 64
N_META = 16
N_A = DEPTH // 2
N_B = DEPTH - N_A
A_INNER = 2 * D_MODEL
A_HEADS = 8
A_HEAD_DIM = A_INNER // A_HEADS
CONV_W = 4
B_HEADS = 16
B_HEAD_DIM = D_MODEL // B_HEADS
B_WIDTH = B_HEADS * B_HEAD_DIM
Q_BLOCK = 128
EPS = 1e-6

kernel_name = "yoco_mlstm_fox_streaming_step"

def rmsnorm(x, g):
    xf = x.astype(jnp.float32)
    y = xf * lax.rsqrt(jnp.mean(jnp.square(xf), axis=-1, keepdims=True) + EPS)
    return (y * g.astype(jnp.float32)).astype(x.dtype)

def head_layernorm(h, g):
    hc = h - jnp.mean(h, axis=-1, keepdims=True)
    return hc * lax.rsqrt(jnp.mean(hc * hc, axis=-1, keepdims=True) + EPS) * g

def causal_conv(x, buf, w, b):
    seq = x.shape[1]
    xp = jnp.concatenate([buf.astype(x.dtype), x], axis=1)
    y = b
    for i in range(CONV_W):
        y = y + xp[:, i:i + seq] * w[i]
    return y, xp[:, -(CONV_W - 1):]

def mlstm_block(state, blk):
    C, n, m = state
    q, k, v, ig, lf = blk
    L = q.shape[2]
    b = jnp.cumsum(lf, axis=-1)
    log_d = b[..., :, None] - b[..., None, :] + ig[..., None, :]
    log_d = jnp.where(jnp.tril(jnp.ones((L, L), dtype=bool)), log_d, -jnp.inf)
    inter = b + m[..., None]
    m_t = jnp.maximum(jnp.max(log_d, axis=-1), inter)
    d = jnp.exp(log_d - m_t[..., None])
    a = jnp.exp(inter - m_t)
    s = jnp.einsum('bhtd,bhsd->bhts', q, k) * d
    num = jnp.einsum('bhts,bhse->bhte', s, v) + a[..., None] * jnp.einsum('bhtd,bhde->bhte', q, C)
    den = jnp.sum(s, axis=-1) + a * jnp.einsum('bhtd,bhd->bht', q, n)
    h = num / jnp.maximum(jnp.abs(den), jnp.exp(-m_t))[..., None]
    m_new = m_t[..., -1]
    decay = jnp.exp(b[..., -1] + m - m_new)
    w = jnp.exp(b[..., -1:] - b + ig - m_new[..., None])
    C_new = decay[..., None, None] * C + jnp.einsum('bhs,bhsd,bhse->bhde', w, k, v)
    n_new = decay[..., None] * n + jnp.einsum('bhs,bhsd->bhd', w, k)
    return (C_new, n_new, m_new), h

def mlstm_run(q, k, v, ig, lf, state, lead):
    if lead == 0:
        state, h = mlstm_block(state, (q, k, v, ig, lf))
        return h, state
    bsz, nh, seq = q.shape[:3]
    state, h0 = mlstm_block(state, (q[:, :, :lead], k[:, :, :lead], v[:, :, :lead], ig[:, :, :lead], lf[:, :, :lead]))
    nc = (seq - lead) // CHUNK

    def to_blocks(t):
        t = t[:, :, lead:]
        return jnp.moveaxis(t.reshape((bsz, nh, nc, CHUNK) + t.shape[3:]), 2, 0)

    state, hs = lax.scan(mlstm_block, state, (to_blocks(q), to_blocks(k), to_blocks(v), to_blocks(ig), to_blocks(lf)))
    hs = jnp.moveaxis(hs, 0, 2).reshape(bsz, nh, seq - lead, A_HEAD_DIM)
    return jnp.concatenate([h0, hs], axis=2), state

def mlstm_layer(x, conv_buf, C, n, m, norm_g, w_in, conv_w, conv_b, wq, wk, wv, w_gate, b_gate, out_g, skip, w_out, lead):
    bsz, seq, _ = x.shape
    xm, z = jnp.split(rmsnorm(x, norm_g) @ w_in, 2, axis=-1)
    xc, new_buf = causal_conv(xm, conv_buf, conv_w, conv_b)
    xc = jax.nn.silu(xc)
    xc_h = xc.reshape(bsz, seq, A_HEADS, A_HEAD_DIM)
    xm_h = xm.reshape(bsz, seq, A_HEADS, A_HEAD_DIM)
    q = jnp.einsum('blhd,hde->blhe', xc_h, wq)
    k = jnp.einsum('blhd,hde->blhe', xc_h, wk) * (A_HEAD_DIM ** -0.5)
    v = jnp.einsum('blhd,hde->blhe', xm_h, wv)
    g_in = jnp.concatenate([q.reshape(bsz, seq, A_INNER), k.reshape(bsz, seq, A_INNER), v.reshape(bsz, seq, A_INNER)], axis=-1)
    gates = (g_in @ w_gate + b_gate).astype(jnp.float32)
    ig = gates[..., :A_HEADS]
    lf = jax.nn.log_sigmoid(gates[..., A_HEADS:])

    def to_bh(t):
        return jnp.moveaxis(t.astype(jnp.float32), 2, 1)

    h, (C, n, m) = mlstm_run(to_bh(q), to_bh(k), to_bh(v), to_bh(ig), to_bh(lf),
                             (C.astype(jnp.float32), n.astype(jnp.float32), m.astype(jnp.float32)), lead)
    h = head_layernorm(jnp.moveaxis(h, 1, 2), out_g.astype(jnp.float32)).reshape(bsz, seq, A_INNER)
    h = (h + skip * xc).astype(x.dtype)
    y = (h * jax.nn.silu(z)) @ w_out
    return x + y.astype(x.dtype), new_buf, C, n, m

def shared_kv(x, kv_norm_g, w_kvf, b_f, k_norm_g):
    bsz, seq, _ = x.shape
    kvf = rmsnorm(x, kv_norm_g) @ w_kvf
    k = rmsnorm(kvf[..., :B_WIDTH].reshape(bsz, seq, B_HEADS, B_HEAD_DIM), k_norm_g)
    v = kvf[..., B_WIDTH:2 * B_WIDTH].reshape(bsz, seq, B_HEADS, B_HEAD_DIM)
    logf = jax.nn.log_sigmoid(kvf[..., 2 * B_WIDTH:].astype(jnp.float32) + b_f.astype(jnp.float32))
    return k, v, logf

def fox_attend(q, f_q, q_pos, k, v, f_k, k_pos):
    s = jnp.einsum('bqhd,bkhd->bhqk', q, k).astype(jnp.float32) * (B_HEAD_DIM ** -0.5)
    s = s + jnp.transpose(f_q, (0, 2, 1))[..., :, None] - jnp.transpose(f_k, (0, 2, 1))[..., None, :]
    s = jnp.where(k_pos[None, :] <= q_pos[:, None], s, -jnp.inf)
    p = jax.nn.softmax(s, axis=-1)
    return jnp.einsum('bhqk,bkhd->bqhd', p.astype(v.dtype), v)

def fox_layer(x, q_pos, f_q, k, v, f_k, k_pos, norm_g, w_in, q_norm_g, w_out, blocked):
    bsz, seq, _ = x.shape
    q, z = jnp.split(rmsnorm(x, norm_g) @ w_in, 2, axis=-1)
    q = rmsnorm(q.reshape(bsz, seq, B_HEADS, B_HEAD_DIM), q_norm_g)
    if blocked:
        nb = seq // Q_BLOCK
        qb = jnp.swapaxes(q.reshape(bsz, nb, Q_BLOCK, B_HEADS, B_HEAD_DIM), 0, 1)
        fb = jnp.swapaxes(f_q.reshape(bsz, nb, Q_BLOCK, B_HEADS), 0, 1)
        pb = q_pos.reshape(nb, Q_BLOCK)
        o = lax.map(lambda blk: fox_attend(blk[0], blk[1], blk[2], k, v, f_k, k_pos), (qb, fb, pb))
        o = jnp.swapaxes(o, 0, 1).reshape(bsz, seq, B_WIDTH)
    else:
        o = fox_attend(q, f_q, q_pos, k, v, f_k, k_pos).reshape(bsz, seq, B_WIDTH)
    y = (o * jax.nn.silu(z)) @ w_out
    return x + y.astype(x.dtype)

def setup_inputs(seed: int = 0) -> dict:
    key = jax.random.key(seed)
    ks = jax.random.split(key, 32)
    f32 = jnp.float32

    def nrm(k, shape, scale):
        return jax.random.normal(k, shape, f32) * scale

    a_b_gate = jnp.concatenate([0.1 * nrm(ks[17], (N_A, A_HEADS), 1.0),
                                jnp.linspace(3.0, 6.0, A_HEADS, dtype=f32)[None] + nrm(ks[18], (N_A, A_HEADS), 0.1)], axis=-1)
    return {
        "x_prompt": nrm(ks[0], (BATCH, SEQ, D_MODEL), 1.0),
        "x_sample": nrm(ks[1], (DEC_BATCH, DEC_SEQ, D_MODEL), 1.0),
        "cache_k": nrm(ks[2], (DEC_BATCH, PAST_LEN, B_HEADS, B_HEAD_DIM), 1.0),
        "cache_v": nrm(ks[3], (DEC_BATCH, PAST_LEN, B_HEADS, B_HEAD_DIM), 1.0),
        "cache_logf": jax.nn.log_sigmoid(3.0 + nrm(ks[4], (DEC_BATCH, PAST_LEN, B_HEADS), 1.0)),
        "state_C": nrm(ks[5], (N_A, DEC_BATCH, A_HEADS, A_HEAD_DIM, A_HEAD_DIM), A_HEAD_DIM ** -0.5),
        "state_n": nrm(ks[6], (N_A, DEC_BATCH, A_HEADS, A_HEAD_DIM), A_HEAD_DIM ** -0.5),
        "state_m": nrm(ks[7], (N_A, DEC_BATCH, A_HEADS), 1.0),
        "state_conv": nrm(ks[8], (N_A, DEC_BATCH, CONV_W - 1, A_INNER), 1.0),
        "meta_tokens": nrm(ks[9], (N_META, D_MODEL), 1.0),
        "a_norm_g": 1.0 + nrm(ks[10], (N_A, D_MODEL), 0.02),
        "a_w_in": nrm(ks[11], (N_A, D_MODEL, 2 * A_INNER), D_MODEL ** -0.5),
        "a_conv_w": nrm(ks[12], (N_A, CONV_W, A_INNER), CONV_W ** -0.5),
        "a_conv_b": nrm(ks[13], (N_A, A_INNER), 0.02),
        "a_wq": nrm(ks[14], (N_A, A_HEADS, A_HEAD_DIM, A_HEAD_DIM), A_HEAD_DIM ** -0.5),
        "a_wk": nrm(ks[15], (N_A, A_HEADS, A_HEAD_DIM, A_HEAD_DIM), A_HEAD_DIM ** -0.5),
        "a_wv": nrm(ks[16], (N_A, A_HEADS, A_HEAD_DIM, A_HEAD_DIM), A_HEAD_DIM ** -0.5),
        "a_w_gate": nrm(ks[19], (N_A, 3 * A_INNER, 2 * A_HEADS), (3 * A_INNER) ** -0.5),
        "a_b_gate": a_b_gate,
        "a_out_g": 1.0 + nrm(ks[20], (N_A, A_HEADS, A_HEAD_DIM), 0.02),
        "a_skip": 1.0 + nrm(ks[21], (N_A, A_INNER), 0.02),
        "a_w_out": nrm(ks[22], (N_A, A_INNER, D_MODEL), A_INNER ** -0.5),
        "kv_norm_g": 1.0 + nrm(ks[23], (D_MODEL,), 0.02),
        "w_kvf": nrm(ks[24], (D_MODEL, 2 * B_WIDTH + B_HEADS), D_MODEL ** -0.5),
        "b_f": jnp.linspace(2.0, 6.0, B_HEADS, dtype=f32) + nrm(ks[25], (B_HEADS,), 0.1),
        "k_norm_g": 1.0 + nrm(ks[26], (B_HEADS, B_HEAD_DIM), 0.02),
        "b_norm_g": 1.0 + nrm(ks[27], (N_B, D_MODEL), 0.02),
        "b_w_in": nrm(ks[28], (N_B, D_MODEL, 2 * B_WIDTH), D_MODEL ** -0.5),
        "q_norm_g": 1.0 + nrm(ks[29], (N_B, B_HEADS, B_HEAD_DIM), 0.02),
        "b_w_out": nrm(ks[30], (N_B, B_WIDTH, D_MODEL), B_WIDTH ** -0.5),
    }

def reference(x_prompt, x_sample, cache_k, cache_v, cache_logf, state_C, state_n, state_m, state_conv,
              meta_tokens, a_norm_g, a_w_in, a_conv_w, a_conv_b, a_wq, a_wk, a_wv, a_w_gate, a_b_gate,
              a_out_g, a_skip, a_w_out, kv_norm_g, w_kvf, b_f, k_norm_g, b_norm_g, b_w_in, q_norm_g, b_w_out):
    bp = x_prompt.shape[0]
    past = cache_k.shape[1]
    dec = x_sample.shape[1]
    f32 = jnp.float32
    xp = jnp.concatenate([jnp.broadcast_to(meta_tokens.astype(x_prompt.dtype)[None], (bp, N_META, D_MODEL)), x_prompt], axis=1)
    xs = x_sample
    p_C, p_n, p_m, p_conv = [], [], [], []
    s_C, s_n, s_m, s_conv = [], [], [], []
    for layer in range(DEPTH):
        if layer < N_A:
            i = layer
            w = (a_norm_g[i], a_w_in[i], a_conv_w[i], a_conv_b[i], a_wq[i], a_wk[i], a_wv[i],
                 a_w_gate[i], a_b_gate[i], a_out_g[i], a_skip[i], a_w_out[i])
            xp, buf, C, n, m = mlstm_layer(
                xp, jnp.zeros((bp, CONV_W - 1, A_INNER), xp.dtype),
                jnp.zeros((bp, A_HEADS, A_HEAD_DIM, A_HEAD_DIM), f32), jnp.zeros((bp, A_HEADS, A_HEAD_DIM), f32),
                jnp.zeros((bp, A_HEADS), f32), *w, N_META)
            p_C.append(C); p_n.append(n); p_m.append(m); p_conv.append(buf)
            xs, buf, C, n, m = mlstm_layer(xs, state_conv[i], state_C[i], state_n[i], state_m[i], *w, 0)
            s_C.append(C); s_n.append(n); s_m.append(m); s_conv.append(buf)
            if layer == N_A - 1:
                p_k, p_v, p_logf = shared_kv(xp, kv_norm_g, w_kvf, b_f, k_norm_g)
                s_k, s_v, s_logf = shared_kv(xs, kv_norm_g, w_kvf, b_f, k_norm_g)
                fp = jnp.cumsum(p_logf, axis=1)
                kpos_p = jnp.arange(fp.shape[1])
                qpos_p = jnp.arange(N_META, fp.shape[1])
                ks_all = jnp.concatenate([cache_k.astype(s_k.dtype), s_k], axis=1)
                vs_all = jnp.concatenate([cache_v.astype(s_v.dtype), s_v], axis=1)
                fs = jnp.cumsum(jnp.concatenate([cache_logf.astype(f32), s_logf], axis=1), axis=1)
                kpos_s = jnp.arange(past + dec)
                qpos_s = jnp.arange(past, past + dec)
                xp = xp[:, N_META:]
        else:
            j = layer - N_A
            xp = fox_layer(xp, qpos_p, fp[:, N_META:], p_k, p_v, fp, kpos_p,
                           b_norm_g[j], b_w_in[j], q_norm_g[j], b_w_out[j], True)
            xs = fox_layer(xs, qpos_s, fs[:, past:], ks_all, vs_all, fs, kpos_s,
                           b_norm_g[j], b_w_in[j], q_norm_g[j], b_w_out[j], False)
    p_C = jnp.stack(p_C); p_n = jnp.stack(p_n); p_m = jnp.stack(p_m); p_conv = jnp.stack(p_conv)
    s_C = jnp.stack(s_C); s_n = jnp.stack(s_n); s_m = jnp.stack(s_m); s_conv = jnp.stack(s_conv)
    return (xp, xs, p_k, p_v, p_logf, p_C, p_n, p_m, p_conv, s_k, s_v, s_logf, s_C, s_n, s_m, s_conv)


_drawn_inputs = setup_inputs


def setup_inputs(seed=0):
    import zlib

    import numpy as np

    out = dict(_drawn_inputs(seed))
    spreads = {}
    factors = {'cache_logf': 3.838,
     'a_out_g': 5.664,
     'a_skip': 8.0,
     'kv_norm_g': 2.853,
     'k_norm_g': 2.896,
     'b_norm_g': 8.0,
     'q_norm_g': 8.0}
    for name, (base, spread) in spreads.items():
        noise = np.random.default_rng([zlib.crc32(name.encode()), seed]).standard_normal(out[name].shape)
        drawn = base * np.exp(spread * noise) if base else spread * noise
        out[name] = jnp.asarray(drawn.astype(out[name].dtype))
    for name, factor in factors.items():
        out[name] = (out[name] * factor).astype(out[name].dtype)
    return out
```

```python
from contextlib import ExitStack

import concourse.bass as bass
from concourse import mybir

F32 = mybir.dt.float32
F32R = mybir.dt.float32r
ALU = mybir.AluOpType
ACT = mybir.ActivationFunctionType
AX = mybir.AxisListType

P = 128
D = 2048
KD = D // P
HEADS = 8
HD = 512
HT = HD // P
INNER = HEADS * HD
META, SEQ, DEC, PAST = 16, 256, 32, 512
TP = META + SEQ
T = TP + DEC
TILES = [(0, 128), (128, 128), (256, T - 256)]
TAIL = T - 256
CONV = 4
PAD = CONV - 1
XW = PAD + TP + PAD + DEC
EPS = 1e-6
NEG = -1e30
SLOTS = 4
CW = 256
GRP = 4
BH = 16
GROUPS = BH // GRP
TQ = T - META
QT = [(0, 128), (128, 128), (256, DEC)]
CONV_N = XW - PAD


class Count:

    def __init__(self, a, b=0, loop=0):
        self.a, self.b, self.loop = a, b, loop

    def __add__(self, k):
        return Count(self.a + k, self.b, self.loop)

    def times(self, k):
        return Count(self.a * k, self.b * k, self.loop)

    def turn(self, n):
        assert self.b % n == 0
        return self.a % n

    def rounds(self, n):
        assert self.b % n == 0
        return Count(self.a // n, self.b // n, self.loop)

    @property
    def value(self):
        return self.loop * self.b + self.a if self.b else self.a


def wait(eng, sem, count):
    if isinstance(count, Count):
        if count.b or count.a > 0:
            eng.wait_ge(sem, count.value)
    elif count > 0:
        eng.wait_ge(sem, count)


class Own:

    def __init__(self, eng, sem, start=0):
        self.eng, self.sem, self.n, self.offset = eng, sem, start, None

    def done(self, instruction):
        instruction.then_inc(self.sem, 1)
        self.n += 1

    def wait(self, back=0):
        n = self.n - back
        self.eng.wait_ge(self.sem, n if self.offset is None else self.offset + n)

    def open(self, loop, per):
        self.offset, self.per, self.at = loop * per, per, self.n

    def close(self, turns):
        assert self.n - self.at == self.per, f"a turn of the loop has {self.n - self.at} own steps"
        self.n += self.per * (turns - 1)
        self.offset = None


def settled(own, cell):
    own.wait()
    own.done(own.eng.tensor_tensor(cell, cell, cell, ALU.mult))


def trunk(nc, i, o):
    whole = ExitStack()
    with whole:
        def sem(name):
            return whole.enter_context(nc.semaphore(name))

        def sb(name, shape, dt=F32, stack=whole):
            return stack.enter_context(nc.sbuf_tensor(name, shape, dt))

        acc = [whole.enter_context(nc.psum_tensor(f"acc{b}", [P, 512], F32)) for b in range(4)]
        aux = [whole.enter_context(nc.psum_tensor(f"aux{b}", [P, 512], F32)) for b in range(4)]

        ident = sb("ident", [P, P])
        ones = sb("ones", [P, P])
        xT = sb("xT", [P, KD, T])
        par = sb("par", [P, 400])
        cell = sb("cell", [1, 1])
        rstd_row = sb("rstd_row", [P, T])
        raw = sb("raw", [P, SLOTS, 4, CW])
        w_hi = sb("w_hi", [P, SLOTS, 4, CW], F32R)
        w_lo = sb("w_lo", [P, SLOTS, 4, CW], F32R)
        CONV_W0, CONV_B0, SKIP0, OUTG0 = 0, 128, 160, 192
        SC0, GA0, GKV0, GB0, N00 = 224, 320, 336, 352, 368

        landed = [sem(f"landed{s}") for s in range(SLOTS)]
        hi_made = sem("hi_made")
        lo_made = sem("lo_made")
        used = sem("used")
        acc_free = [sem(f"acc_free{b}") for b in range(4)]
        dve_own = sem("dve_own")
        act_own = sem("act_own")
        pool_own = sem("pool_own")

        def load_chunk(sp, n, src):
            s = n.turn(SLOTS)
            wait(sp, lo_made, n + (1 - SLOTS))
            sp.dma_start(raw[:, s, :, :], src.rearrange("(k p) c -> p k c", p=P)).then_inc(landed[s], 16)

        def high_part(act, n):
            s = n.turn(SLOTS)
            wait(act, landed[s], (n.rounds(SLOTS) + 1).times(16))
            wait(act, used, n + (1 - SLOTS))
            act.activation(w_hi[:, s, :, :], raw[:, s, :, :], ACT.Copy).then_inc(hi_made, 1)

        def low_part(dve, n):
            s = n.turn(SLOTS)
            wait(dve, hi_made, n + 1)
            dve.tensor_tensor(w_lo[:, s, :, :], raw[:, s, :, :], w_hi[:, s, :, :].bitcast(F32),
                              ALU.subtract).then_inc(lo_made, 1)

        def products(pe, n, tile, x_hi, x_lo, k0, first, last):
            s = n.turn(SLOTS)
            wait(pe, lo_made, n + 1)
            for m in range(2):
                u = tile + m
                b = u.turn(4)
                width = x_hi.shape[-1]
                if first:
                    wait(pe, acc_free[b], u.rounds(4))
                for k in range(4):
                    wh = w_hi[:, s, k, m * P:(m + 1) * P]
                    wl = w_lo[:, s, k, m * P:(m + 1) * P]
                    st = first and k == 0
                    pe.matmul(acc[b][:, 0:width], wh, x_hi[:, k0 + k, :], start=st, stop=False)
                    pe.matmul(acc[b][:, 0:width], wh, x_lo[:, k0 + k, :], start=False, stop=False)
                    mm = pe.matmul(acc[b][:, 0:width], wl, x_hi[:, k0 + k, :], start=False,
                                   stop=last and k == 3)
            mm.then_inc(used, 1)

        C_MIX = 8 + 14 * (HEADS - 1) + 6
        A_MIX = 16 * HEADS
        X_MIX = 8 * HEADS

        ph = whole.enter_context(ExitStack())
        xg_hi = sb("xg_hi", [P, KD, T], F32R, ph)
        xg_lo = sb("xg_lo", [P, KD, T], F32R, ph)
        S_raw = sb("S_raw", [P, HEADS, 528], F32, ph)
        q_new = sb("q_new", [P, HEADS, HT, DEC], F32, ph)
        conv_end = sb("conv_end", [P, 2, PAD, 32], F32, ph)
        gate_sum = aux[3]

        p0 = ExitStack()
        x_tok = sb("x_tok", [P, 3, D], F32, p0)
        sq_junk = sb("sq_junk", [P, D], F32, p0)
        rows = sb("rows", [P, 4, P], F32, p0)
        small = sb("small", [P, 8, 3], F32, p0)
        diag = sb("diag", [P, 3, P], F32, p0)
        p0.close()

        x_in, par_in = sem("x_in"), sem("par_in")
        id_zero, id_set = sem("id_zero"), sem("id_set")
        turned, taken = sem("turned"), sem("taken")
        par_turned, par_taken = sem("par_turned"), sem("par_taken")
        x_hi_made = sem("x_hi_made")
        ss_ready, mean_ready, ln_ready = sem("ss_ready"), sem("mean_ready"), sem("ln_ready")
        diag_ready, bcast_ready = sem("diag_ready"), sem("bcast_ready")
        inv_count = sem("inv_count")
        prep_done = sem("prep_done")

        def newton(dve, own, y, v, t):
            own.done(dve.tensor_tensor(t, y, y, ALU.mult))
            own.wait()
            own.done(dve.tensor_tensor(t, t, v, ALU.mult))
            own.wait()
            own.done(dve.tensor_scalar(t, t, -0.5, 1.5, ALU.mult, ALU.add))
            own.wait()
            own.done(dve.tensor_tensor(y, y, t, ALU.mult))
            own.wait()

        with nc.Block() as block:
            @block.sync
            def _(sp):
                for j in range(SLOTS):
                    load_chunk(sp, Count(j), i["a_w_in"][0, 512 * j:512 * (j + 1), 0:CW])

            @block.scalar
            def _(act):
                act.dma_start(x_tok[0:META, 0, :], i["meta_tokens"]).then_inc(x_in, 16)
                act.dma_start(x_tok[META:P, 0, :], i["x_prompt"][0, 0:112, :]).then_inc(x_in, 16)
                act.dma_start(x_tok[:, 1, :], i["x_prompt"][0, 112:240, :]).then_inc(x_in, 16)
                act.dma_start(x_tok[0:16, 2, :], i["x_prompt"][0, 240:256, :]).then_inc(x_in, 16)
                act.dma_start(x_tok[16:TAIL, 2, :], i["x_sample"][0]).then_inc(x_in, 16)
                own = Own(act, act_own)
                act.wait_ge(x_in, 80)
                act.wait_ge(prep_done, 1)
                for t, (_, n) in enumerate(TILES):
                    own.done(act.activation(sq_junk[0:n, :], x_tok[0:n, t, :], ACT.Square,
                                            accum_out=small[0:n, 0, t:t + 1]))
                    own.wait()
                act.activation(small[:, 1, :], small[:, 0, :], ACT.Copy, scale=1.0 / D).then_inc(ss_ready, 1)
                act.wait_ge(mean_ready, 1)
                own.done(act.activation(small[:, 3, :], small[:, 2, :], ACT.Ln))
                own.wait()
                act.activation(small[:, 4, :], small[:, 3, :], ACT.Exp, scale=-0.5).then_inc(ln_ready, 1)
                act.wait_ge(par_taken, 1)
                for k in range(KD):
                    act.wait_ge(taken, k + 1)
                    act.activation(xg_hi[:, k, :], xT[:, k, :], ACT.Copy,
                                   scale=par[:, GA0 + k:GA0 + k + 1]).then_inc(x_hi_made, 1)

            @block.gpsimd
            def _(pool):
                for r, (name, src) in enumerate([
                        ("conv_w", i["a_conv_w"][0].rearrange("j (m p) -> j m p", p=P)),
                        ("conv_b", i["a_conv_b"].rearrange("a (m p) -> (a m) p", p=P)),
                        ("skip", i["a_skip"].rearrange("a (m p) -> (a m) p", p=P)),
                        ("out_g", i["a_out_g"][0].rearrange("h (m p) -> h m p", p=P)),
                        ("state", i["state_conv"][0, 0].rearrange("j (m p) -> j m p", p=P)),
                        ("a_norm", i["a_norm_g"].rearrange("a (m p) -> (a m) p", p=P)),
                        ("kv_norm", i["kv_norm_g"].rearrange("(m p) -> m p", p=P)),
                        ("b_norm", i["b_norm_g"].rearrange("a (m p) -> (a m) p", p=P)),
                        ("n0", i["state_n"][0, 0].rearrange("h (m p) -> h m p", p=P))]):
                    tile, row, count = [(0, 0, 128), (1, 0, 32), (1, 32, 32), (1, 64, 32), (2, 0, 96),
                                        (3, 0, 16), (3, 16, 16), (3, 32, 16), (3, 48, 32)][r]
                    if len(src.shape) == 3:
                        src = src.rearrange("a b c -> (a b) c")
                    pool.dma_start(rows[row:row + count, tile, :], src).then_inc(par_in, 16)
                pool.memset(cell[:, :], 0.0).then_inc(pool_own, 1)
                pool.memset(ident[:, :], 0.0).then_inc(id_zero, 1)
                pool.wait_ge(id_zero, 1)
                pool.affine_select(out=ident[:, :], in_=ident[:, :], compare_op=ALU.not_equal, fill=1.0,
                                   base=0, pattern=[[-1, P]], channel_multiplier=1).then_inc(id_set, 1)

            @block.tensor
            def _(pe):
                pe.wait_ge(id_set, 1)
                pe.wait_ge(x_in, 80)
                for k in range(KD):
                    if k >= 4:
                        pe.wait_ge(taken, k - 3)
                    for t, (t0, n) in enumerate(TILES):
                        mm = pe.transpose(acc[k % 4][:, t0:t0 + n], x_tok[0:n, t, k * P:(k + 1) * P],
                                          ident[0:n, 0:n])
                    mm.then_inc(turned, 1)
                    if k == 1:
                        pe.wait_ge(par_in, 16 * 9)
                        for r, (c0, n) in enumerate([(0, 128), (128, 96), (224, 96), (320, 80)]):
                            mm = pe.transpose(aux[0][:, c0:c0 + n], rows[0:n, r, :], ident[0:n, 0:n])
                        mm.then_inc(par_turned, 1)
                pe.wait_ge(diag_ready, 1)
                for t, (t0, n) in enumerate(TILES):
                    mm = pe.matmul(aux[1][:, t0:t0 + n], ones[0:n, :], diag[0:n, t, 0:n], start=True, stop=True)
                mm.then_inc(bcast_ready, 1)

            @block.vector
            def _(dve):
                own = Own(dve, dve_own)
                dve.memset(small[:, :, :], 1.0).then_inc(prep_done, 1)
                own.done(dve.memset(ones[:, :], 1.0))

                def low(k):
                    dve.wait_ge(x_hi_made, k + 1)
                    dve.scalar_tensor_tensor(xg_lo[:, k, :], xT[:, k, :], par[:, GA0 + k:GA0 + k + 1],
                                             xg_hi[:, k, :].bitcast(F32), ALU.mult, ALU.subtract)

                for k in range(KD):
                    dve.wait_ge(turned, k + 1)
                    dve.tensor_copy(xT[:, k, :], acc[k % 4][:, 0:T]).then_inc(taken, 1)
                    if k == 1:
                        dve.wait_ge(par_turned, 1)
                        dve.tensor_copy(par[:, :], aux[0][:, 0:400]).then_inc(par_taken, 1)
                dve.wait_ge(ss_ready, 1)
                dve.tensor_scalar(small[:, 2, :], small[:, 1, :], EPS, None, ALU.add).then_inc(mean_ready, 1)
                dve.wait_ge(par_taken, 1)
                dve.wait_ge(ln_ready, 1)
                dve.wait_ge(mean_ready, 1)
                newton(dve, own, small[:, 4, :], small[:, 2, :], small[:, 5, :])
                dve.wait_ge(id_set, 1)
                for t, (_, n) in enumerate(TILES):
                    ins = dve.tensor_scalar(diag[0:n, t, :], ident[0:n, :], small[0:n, 4, t:t + 1], None, ALU.mult)
                ins.then_inc(diag_ready, 1)
                dve.wait_ge(taken, KD)
                for k in range(KD):
                    low(k)
                dve.wait_ge(bcast_ready, 1)
                own.done(dve.tensor_copy(rstd_row[:, :], aux[1][:, 0:T]))
                own.wait()
        own_dve0, own_act0 = 1 + 4 + 1, 4

        p1 = ExitStack()
        xm = sb("xm", [P, HT, XW], F32, p1)
        cv = sb("cv", [P, HT, CONV_N], F32, p1)
        xc = sb("xc", [P, HT, T], F32, p1)
        xm_hi, xm_lo = sb("xm_hi", [P, HT, T], F32R, p1), sb("xm_lo", [P, HT, T], F32R, p1)
        xc_hi, xc_lo = sb("xc_hi", [P, HT, T], F32R, p1), sb("xc_lo", [P, HT, T], F32R, p1)
        q_T, k_T, v_T = (sb(n, [P, HT, T], F32, p1) for n in ("q_T", "k_T", "v_T"))
        k_tok, v_tok = sb("k_tok", [P, 3, HD], F32, p1), sb("v_tok", [P, 3, HD], F32, p1)
        skipped = sb("skipped", [P, HT, T], F32, p1)
        wg_in = sb("wg_in", [P, 12, 16], F32, p1)
        wg = sb("wg", [P, 12, 40], F32, p1)
        zero_w = sb("zero_w", [P, 40], F32, p1)
        p1.close()
        k_dram = nc.dram_tensor("k_scratch", (HEADS, T, HD), F32, kind="Internal").ap()
        v_dram = nc.dram_tensor("v_scratch", (HEADS, T, HD), F32, kind="Internal").ap()
        s_dram = nc.dram_tensor("skip_scratch", (HEADS, P, HT, T), F32, kind="Internal").ap()

        conv_made, xc_made, xm_hi_made, qkv_ready = (sem(n) for n in ("conv_made", "xc_made", "xm_hi_made", "qkv_ready"))
        post_ready = sem("post_ready")
        post_free = [sem(f"post_free{b}") for b in range(2)]
        k_stored, v_stored, skip_stored = sem("k_stored"), sem("v_stored"), sem("skip_stored")
        wg_landed, wg_ready = sem("wg_landed"), sem("wg_ready")
        mix_set, silu_made = sem("mix_set"), sem("silu_made")
        MIX_OWN, M_OWN, counted = 2 * (4 * 3 + 2), 17, {}
        HPT = 2
        LOOPS = (HEADS - 2) // HPT

        def z_load(sp, n, h, j):
            col = h.times(HD) + (INNER + CW * (j // 4))
            load_chunk(sp, n, i["a_w_in"][0, 512 * (j % 4):512 * (j % 4 + 1), bass.ds(col.value, CW)])

        with nc.Block() as block:
            def xm_chunk(h, j):
                return h.times(14) + (8 + j)

            def qkv_chunk(h, j):
                return h.times(14) + (8 + 8 + j)

            @block.sync
            def _(sp):
                def xm_load(n, h, j):
                    col = h.times(HD) + CW * (j // 4)
                    src = i["a_w_in"][0, 512 * (j % 4):512 * (j % 4 + 1), bass.ds(col.value, CW)]
                    load_chunk(sp, n, src)

                def qkv_load(n, h, j):
                    w = (i["a_wq"], i["a_wk"], i["a_wv"])[j // 2]
                    src = w[0].rearrange("h r c -> (h r) c")[bass.ds(h.times(HD).value, HD),
                                                             CW * (j % 2):CW * (j % 2 + 1)]
                    load_chunk(sp, n, src)

                for j in range(SLOTS, 8):
                    xm_load(Count(j), Count(0), j)

                def turn(h):
                    for j in range(8):
                        xm_load(xm_chunk(h, j), h + 1, j)
                    for j in range(6):
                        qkv_load(qkv_chunk(h, j), h, j)

                turn(Count(0))
                with sp.Fori(0, LOOPS) as it:
                    for p in range(HPT):
                        turn(Count(1 + p, HPT, it))
                h = Count(HEADS - 1)
                for j in range(6):
                    qkv_load(xm_chunk(h, j), h, j)
                for j in range(SLOTS):
                    z_load(sp, Count(C_MIX + j), Count(0), j)

            def steps(h, last):
                if last:
                    return [(xm_chunk(h, j), 8 + j) for j in range(6)]
                return [(xm_chunk(h, j), j) for j in range(8)] + [(qkv_chunk(h, j), 8 + j) for j in range(6)]

            def tile_of(h, j, last):
                if j < 8:
                    return h.times(16) + (4 + 2 * (j // 4))
                return h.times(16) + ((4 if last else 8) + 2 * (j - 8))

            @block.scalar
            def _(act):
                def convolved(h, m):
                    wait(act, conv_made, h.times(HT) + (m + 1))
                    act.activation(xc[:, m, 0:TP], cv[:, m, 0:TP], ACT.Silu)
                    act.activation(xc[:, m, TP:T], cv[:, m, TP + PAD:CONV_N], ACT.Silu).then_inc(silu_made, 1)
                    wait(act, used, h.times(14) + 8)
                    act.activation(xm_hi[:, m, 0:TP], xm[:, m, PAD:PAD + TP], ACT.Copy)
                    act.activation(xm_hi[:, m, TP:T], xm[:, m, XW - DEC:XW], ACT.Copy)
                    wait(act, silu_made, h.times(HT) + (m + 1))
                    act.activation(xc_hi[:, m, :], xc[:, m, :], ACT.Copy).then_inc(xc_made, 1)

                def by_token(h, pieces=range(2, 8)):
                    for k in pieces:
                        u = h.times(8) + k
                        wait(act, post_ready, u + 1)
                        dst, stored = ((k_tok, k_stored), (v_tok, v_stored))[(k - 2) // 3]
                        t = (k - 2) % 3
                        if t == 0:
                            wait(act, stored, h.times(32))
                        n = TILES[t][1]
                        act.activation(dst[0:n, t, :], aux[u.turn(2)][0:n, :],
                                       ACT.Copy).then_inc(post_free[u.turn(2)], 1)

                def take_qkv(h, n, j, tile):
                    for m in range(2):
                        u = tile + m
                        src = acc[u.turn(4)]
                        wait(act, used, n + 1)
                        d = 2 * (j % 2) + m
                        dst = (q_T, k_T, v_T)[(j - 8) // 2]
                        if dst is q_T:
                            act.activation(q_new[:, h.value, d, :], src[:, TP:T], ACT.Copy)
                        act.activation(dst[:, d, :], src[:, 0:T], ACT.Copy,
                                       scale=HD ** -0.5 if dst is k_T else 1.0).then_inc(acc_free[u.turn(4)], 1)

                def turn(h, first=False, last=False):
                    if last:
                        by_token(h + -1)
                        for m in range(HT):
                            convolved(h, m)
                    for n, j in steps(h, last):
                        high_part(act, n + 2)
                        if 1 <= j < 5:
                            convolved(h, j - 1)
                        if 4 <= j < 7 and not first:
                            by_token(h + -1, (2 * j - 6, 2 * j - 5))
                        if j >= 8:
                            take_qkv(h, n, j, tile_of(h, j, last))

                high_part(act, Count(0))
                high_part(act, Count(1))
                for j in range(8):
                    high_part(act, Count(j + 2))
                turn(Count(0), first=True)
                with act.Fori(0, LOOPS) as it:
                    for p in range(HPT):
                        turn(Count(1 + p, HPT, it))
                turn(Count(HEADS - 1), last=True)
                by_token(Count(HEADS - 1))

            @block.vector
            def _(dve):
                dve.memset(zero_w[:, :], 0.0)
                dve.memset(wg[:, :, :], 0.0)
                dve.memset(xm[:, :, 0:PAD], 0.0).then_inc(mix_set, 1)

                def take_xm(h, m0, n, tile):
                    wait(dve, qkv_ready, h.times(HT) + (m0 - 2))
                    for m in (m0, m0 + 1):
                        u = tile + (m - m0)
                        wait(dve, used, n + 1)
                        dve.tensor_tensor(xm[:, m, PAD:PAD + TP], acc[u.turn(4)][:, 0:TP], rstd_row[:, 0:TP], ALU.mult)
                        dve.tensor_tensor(xm[:, m, XW - DEC:XW], acc[u.turn(4)][:, TP:T], rstd_row[:, TP:T],
                                          ALU.mult).then_inc(acc_free[u.turn(4)], 1)
                    wait(dve, acc_free[u.turn(4)], u.rounds(4) + 1)
                    tiles = bass.ds((h.times(HT) + m0).value, 2)
                    state = par[:, SC0:SC0 + 96].rearrange("p (j m) -> p m j", m=32)
                    end = conv_end[:, :, :, :].rearrange("p s j m -> p s m j")
                    dve.tensor_copy(end[:, 0, tiles, :], xm[:, m0:m0 + 2, TP:TP + PAD])
                    dve.tensor_copy(end[:, 1, tiles, :], xm[:, m0:m0 + 2, XW - PAD:XW])
                    own.done(dve.tensor_copy(xm[:, m0:m0 + 2, PAD + TP:PAD + TP + PAD], state[:, tiles, :]))

                def convolve(h, m):
                    own.wait()
                    tile = h.times(HT) + m
                    for j in range(CONV):
                        w = par[:, bass.ds((tile + (CONV_W0 + 32 * j)).value, 1)]
                        if j == 0:
                            b = par[:, bass.ds((tile + CONV_B0).value, 1)]
                            ins = dve.tensor_scalar(cv[:, m, :], xm[:, m, 0:CONV_N], w, b, ALU.mult, ALU.add)
                        else:
                            ins = dve.scalar_tensor_tensor(cv[:, m, :], xm[:, m, j:j + CONV_N], w, cv[:, m, :],
                                                           ALU.mult, ALU.add)
                        if j < CONV - 1:
                            own.done(ins)
                            own.wait()
                    ins.then_inc(conv_made, 1)

                def finish(h, m):
                    wait(dve, xc_made, h.times(HT) + (m + 1))
                    if m == 0:
                        wait(dve, skip_stored, h.times(16))
                    dve.tensor_tensor(xm_lo[:, m, 0:TP], xm[:, m, PAD:PAD + TP], xm_hi[:, m, 0:TP].bitcast(F32),
                                      ALU.subtract)
                    dve.tensor_tensor(xm_lo[:, m, TP:T], xm[:, m, XW - DEC:XW], xm_hi[:, m, TP:T].bitcast(F32),
                                      ALU.subtract)
                    dve.tensor_scalar(skipped[:, m, :], xc[:, m, :],
                                      par[:, bass.ds((h.times(HT) + (SKIP0 + m)).value, 1)], None, ALU.mult)
                    dve.tensor_tensor(xc_lo[:, m, :], xc[:, m, :], xc_hi[:, m, :].bitcast(F32),
                                      ALU.subtract).then_inc(qkv_ready, 1)

                def gate_weights(h):
                    wait(dve, wg_landed, (h + 1).times(48))
                    wait(dve, post_ready, h.times(8))
                    dve.tensor_copy(wg[:, :, 0:8], wg_in[:, :, 0:8])
                    dve.tensor_copy(wg[:, :, 32:40], wg_in[:, :, 8:16]).then_inc(wg_ready, 1)

                def take_pairs(h):
                    wait(dve, post_ready, h.times(8) + 1)
                    dve.tensor_copy(S_raw[:, h.value, 0:T], aux[0][:, 0:T]).then_inc(post_free[0], 1)
                    wait(dve, post_ready, h.times(8) + 2)
                    dve.tensor_copy(S_raw[:, h.value, T:480], aux[1][:, 0:T - P])
                    dve.tensor_copy(S_raw[0:TAIL, h.value, 480:528], aux[1][0:TAIL, T - P:T - P + TAIL])\
                       .then_inc(post_free[1], 1)

                def turn(h, first=False, last=False):
                    if last:
                        gate_weights(h + -1)
                        take_pairs(h + -1)
                        for m in range(HT):
                            finish(h, m)
                    for n, j in steps(h, last):
                        low_part(dve, n + 2)
                        if 2 <= j < 6:
                            finish(h, j - 2)
                        if 8 <= j < 12 and not last:
                            convolve(h + 1, j - 8)
                        if j == 2 and not first:
                            gate_weights(h + -1)
                        if j == 3:
                            take_xm(h + 1, 0, n, tile_of(h, 0, last))
                        if j == 4 and not first:
                            take_pairs(h + -1)
                        if j == 7:
                            take_xm(h + 1, 2, n, tile_of(h, 4, last))

                own = Own(dve, dve_own, own_dve0)
                own.wait()
                low_part(dve, Count(0))
                low_part(dve, Count(1))
                for j in range(8):
                    low_part(dve, Count(j + 2))
                    if j in (3, 7):
                        take_xm(Count(0), 2 * (j // 4), Count(j), Count(2 * (j // 4)))
                for m in range(HT):
                    convolve(Count(0), m)
                turn(Count(0), first=True)
                with dve.Fori(0, LOOPS) as it:
                    own.open(it, MIX_OWN)
                    for p in range(HPT):
                        turn(Count(1 + p, HPT, it))
                    own.close(LOOPS)
                turn(Count(HEADS - 1), last=True)
                gate_weights(Count(HEADS - 1))
                take_pairs(Count(HEADS - 1))
                counted["dve"] = own.n

            @block.tensor
            def _(pe):
                def gate_products(h, k):
                    x = (q_T, k_T, v_T)[k // 4][:, k % 4, :]
                    pe.matmul(gate_sum[0:40, 0:T], wg[:, k, :], x, start=False, stop=False, skip_group_check=True)

                def post(h, last, pieces=range(8)):
                    if 0 in pieces:
                        for b in range(4):
                            wait(pe, acc_free[b], h.times(4) + (4 if last else 5))
                        wait(pe, wg_ready, h + 1)
                    for k in pieces:
                        u = h.times(8) + k
                        b = u.turn(2)
                        wait(pe, post_free[b], u.rounds(2))
                        if k < 2:
                            for t in ((0,), (1, 2))[k]:
                                t0, n = TILES[t]
                                c = 0 if t < 2 else T - P
                                for d in range(HT):
                                    mm = pe.matmul(aux[b][0:n, c:c + T - t0], k_T[:, d, t0:t0 + n], q_T[:, d, t0:T],
                                                   start=d == 0, stop=d == HT - 1)
                        else:
                            for g in (2 * k - 4, 2 * k - 3):
                                gate_products(h, g)
                            t0, n = TILES[(k - 2) % 3]
                            for d in range(HT):
                                mm = pe.transpose(aux[b][0:n, d * P:(d + 1) * P],
                                                  (k_T, v_T)[(k - 2) // 3][:, d, t0:t0 + n], ident[:, :])
                        mm.then_inc(post_ready, 1)

                def turn(h, first=False, last=False):
                    for n, j in steps(h, last):
                        if 4 <= j < 8 and not first:
                            post(h + -1, False, (2 * j - 8, 2 * j - 7))
                        if j < 8:
                            products(pe, n, tile_of(h, j, last), xg_hi, xg_lo, 4 * (j % 4), j % 4 == 0, j % 4 == 3)
                        else:
                            wait(pe, qkv_ready, (h + 1).times(HT))
                            x = (xc_hi, xc_lo) if j < 12 else (xm_hi, xm_lo)
                            products(pe, n, tile_of(h, j, last), *x, 0, True, True)

                pe.wait_ge(mix_set, 1)
                pe.matmul(gate_sum[0:40, 0:T], zero_w[:, :], xT[:, 0, :], start=True, stop=False,
                          skip_group_check=True)
                for j in range(8):
                    products(pe, Count(j), Count(2 * (j // 4)), xg_hi, xg_lo, 4 * (j % 4), j % 4 == 0, j % 4 == 3)
                turn(Count(0), first=True)
                with pe.Fori(0, LOOPS) as it:
                    for p in range(HPT):
                        turn(Count(1 + p, HPT, it))
                post(Count(HEADS - 2), False)
                turn(Count(HEADS - 1), last=True)
                post(Count(HEADS - 1), True)

            @block.gpsimd
            def _(pool):
                gate_rows = i["a_w_gate"][0].rearrange("(g h k p) c -> g h p k c", g=3, k=HT, p=P)

                def gates_in(h):
                    for g in range(3):
                        pool.dma_start(wg_in[:, 4 * g:4 * g + 4, :], gate_rows[g, h.value]).then_inc(wg_landed, 16)

                def store_tokens(h):
                    wait(pool, post_free[0], h.times(4) + 4)
                    wait(pool, post_free[1], h.times(4) + 4)
                    settled(own, cell[:, :])
                    for src, dst, stored in ((k_tok, k_dram, k_stored), (v_tok, v_dram, v_stored)):
                        rows_ = dst.rearrange("h t c -> h t c")
                        pool.dma_start(rows_[h.value, 0:256, :].rearrange("(t p) c -> p t c", p=P), src[:, 0:2, :])\
                            .then_inc(stored, 16)
                        pool.dma_start(rows_[h.value, 256:T, :], src[0:TAIL, 2, :]).then_inc(stored, 16)

                def turn(h, first=False, last=False):
                    if not first:
                        wait(pool, wg_ready, h)
                        settled(own, cell[:, :])
                        gates_in(h)
                    wait(pool, qkv_ready, h.times(HT) + HT)
                    settled(own, cell[:, :])
                    pool.dma_start(s_dram[h.value], skipped[:, :, :]).then_inc(skip_stored, 16)
                    if not first:
                        store_tokens(h + -1)

                own = Own(pool, pool_own, 1)
                gates_in(Count(0))
                turn(Count(0), first=True)
                with pool.Fori(0, LOOPS) as it:
                    own.open(it, 3 * HPT)
                    for p in range(HPT):
                        turn(Count(1 + p, HPT, it))
                    own.close(LOOPS)
                turn(Count(HEADS - 1), last=True)
                store_tokens(Count(HEADS - 1))
                wait(pool, skip_stored, 16 * HEADS)
                wait(pool, k_stored, 32 * HEADS)
                wait(pool, v_stored, 32 * HEADS)
                counted["pool"] = own.n

        cols = sb("cols", [P, 3, P], F32, ph)
        U_COL, EM_COL, WP_COL, WS_COL = 0, 32, 64, 96
        negM = sb("negM", [P, HEADS, T], F32, ph)
        a_row = sb("a_row", [P, HEADS, DEC], F32, ph)
        mask = sb("mask", [P, 528], F32, ph)
        n_all = sb("n_all", [P, 2, HEADS, HT], F32, ph)

        pg = ExitStack()
        row = {name: sb(f"row_{name}", [HEADS, T], F32, pg) for name in
               ("ig", "g", "abs", "e", "l", "lf", "F", "u", "M", "m")}
        turned_rows = sb("turned_rows", [P, T], F32, pg)
        spread = sb("spread", [40, T], F32, pg)
        pick = sb("pick", [40, HEADS, P], F32, pg)
        bias = sb("bias", [40, 1], F32, pg)
        m0 = sb("m0", [HEADS, 1], F32, pg)
        conv_out = sb("conv_out", [96, 2, P], F32, pg)
        pg.close()
        g_in, g_set, g_dve, g_act, g_pe, g_out = (sem(n) for n in ("g_in", "g_set", "g_dve", "g_act", "g_pe", "g_out"))
        g_mask, g_cols = sem("g_mask"), sem("g_cols")

        with nc.Block() as block:
            @block.gpsimd
            def _(pool):
                pool.dma_start(bias[0:8, :], i["a_b_gate"][0, 0:8].rearrange("(p a) -> p a", a=1)).then_inc(g_in, 16)
                pool.dma_start(bias[32:40, :], i["a_b_gate"][0, 8:16].rearrange("(p a) -> p a", a=1)).then_inc(g_in, 16)
                pool.dma_start(m0[:, :], i["state_m"][0, 0].rearrange("(p a) -> p a", a=1)).then_inc(g_in, 16)
                for k, (part, parts, c0, c1, stop) in enumerate([(mask, P, 0, T, TP), (mask, P, T, 480, 480 - DEC),
                                                                 (mask, TAIL, 480, 528, 528)]):
                    m = mask[0:parts, c0:c1]
                    pool.memset(m, 0.0).then_inc(g_mask, 1)
                    pool.wait_ge(g_mask, 3 * k + 1)
                    pool.affine_select(out=m, in_=m, compare_op=ALU.is_ge, fill=NEG, base=0,
                                       pattern=[[1, c1 - c0]], channel_multiplier=-1).then_inc(g_mask, 1)
                    pool.wait_ge(g_mask, 3 * k + 2)
                    if k < 2:
                        pool.memset(mask[:, stop:c1], NEG).then_inc(g_mask, 1)
                    else:
                        pool.memset(mask[0:16, 480 + 16:528], NEG).then_inc(g_mask, 1)
                    pool.wait_ge(g_mask, 3 * k + 3)
                pool.wait_ge(g_act, 6)
                pool.dma_start(o["p_m"][0, 0].rearrange("(p a) -> p a", a=1), row["m"][:, TP - 1:TP]).then_inc(g_out, 16)
                pool.dma_start(o["s_m"][0, 0].rearrange("(p a) -> p a", a=1), row["m"][:, T - 1:T]).then_inc(g_out, 16)
                pool.wait_ge(g_cols, 2)
                pool.dma_start(o["p_conv"][0, 0].rearrange("j (m p) -> (j m) p", p=P), conv_out[:, 0, :]).then_inc(g_out, 16)
                pool.dma_start(o["s_conv"][0, 0].rearrange("j (m p) -> (j m) p", p=P), conv_out[:, 1, :]).then_inc(g_out, 16)
                pool.wait_ge(g_out, 64)

            @block.vector
            def _(dve):
                own = Own(dve, dve_own, counted["dve"])

                def step(ins):
                    own.done(ins)
                    own.wait()

                step(dve.memset(cols[:, :, :], 1.0))
                step(dve.memset(turned_rows[:, :], 0.0))
                step(dve.memset(spread[:, :], 0.0))
                for q0 in (0, 32):
                    step(dve.tensor_copy(pick[q0:q0 + 8, :, :],
                                         ident[q0:q0 + 8, q0:q0 + 8].unsqueeze(2).to_broadcast([8, HEADS, P])))
                dve.wait_ge(g_in, 48)
                r = {k: v[:, :] for k, v in row.items()}
                step(dve.tensor_scalar(r["ig"], gate_sum[0:8, 0:T], bias[0:8, :], None, ALU.add))
                step(dve.tensor_scalar(r["g"], gate_sum[32:40, 0:T], bias[32:40, :], None, ALU.add))
                dve.scalar_tensor_tensor(r["abs"], r["g"], -1.0, r["g"], ALU.mult, ALU.max).then_inc(g_dve, 1)
                dve.wait_ge(g_act, 2)
                step(dve.scalar_tensor_tensor(r["lf"], r["g"], 0.0, r["l"], ALU.min, ALU.subtract))
                for t0, t1 in ((0, TP), (TP, T)):
                    step(dve.tensor_tensor_scan(row["F"][:, t0:t1], ones[0:8, 0:1].to_broadcast([8, t1 - t0]),
                                                row["lf"][:, t0:t1], 0.0, ALU.mult, ALU.add))
                step(dve.tensor_tensor(r["u"], r["ig"], r["F"], ALU.subtract))
                step(dve.tensor_tensor_scan(row["M"][:, 0:TP], row["u"][:, 0:TP], row["u"][:, 0:TP], 0.0, ALU.max, ALU.max))
                step(dve.tensor_tensor_scan(row["M"][:, TP:T], row["u"][:, TP:T], row["u"][:, TP:T], m0[:, 0:1],
                                            ALU.max, ALU.max))
                step(dve.tensor_tensor(r["m"], r["F"], r["M"], ALU.add))
                step(dve.tensor_copy(turned_rows[0:8, :], r["u"]))
                dve.tensor_scalar(spread[0:8, :], r["M"], -1.0, None, ALU.mult).then_inc(g_dve, 1)
                dve.wait_ge(g_pe, 1)
                for t, (_, n) in enumerate(TILES):
                    ins = dve.tensor_copy(cols[0:n, t, :], aux[0][0:n, t * P:(t + 1) * P])
                ins.then_inc(g_cols, 1)
                dve.wait_ge(g_pe, 2)
                dve.tensor_copy(conv_out[:, :, :], aux[1][0:96, 0:256]).then_inc(g_cols, 1)
                dve.wait_ge(g_pe, 3)
                dve.tensor_copy(a_row[:, :, :], aux[2][:, 0:HEADS * DEC]).then_inc(g_cols, 1)
                for h in range(HEADS):
                    dve.wait_ge(g_pe, 4 + h)
                    dve.tensor_copy(negM[:, h, :], acc[h % 4][:, 0:T]).then_inc(g_cols, 1)
                dve.wait_ge(g_cols, 3 + HEADS)
                counted["dve"] = own.n

            @block.scalar
            def _(act):
                act.wait_ge(g_dve, 1)
                act.activation(row["e"][:, :], row["abs"][:, :], ACT.Exp, scale=-1.0).then_inc(g_act, 1)
                act.wait_ge(g_act, 1)
                act.activation(row["l"][:, :], row["e"][:, :], ACT.Ln, bias=1.0).then_inc(g_act, 1)
                act.wait_ge(g_dve, 2)
                act.activation(turned_rows[32:40, :], row["m"][:, :], ACT.Exp, scale=-1.0).then_inc(g_act, 1)
                act.activation(turned_rows[64:72, 0:TP], row["u"][:, 0:TP], ACT.Exp,
                               bias=spread[0:8, TP - 1:TP]).then_inc(g_act, 1)
                act.activation(turned_rows[96:104, TP:T], row["u"][:, TP:T], ACT.Exp,
                               bias=spread[0:8, T - 1:T]).then_inc(g_act, 1)
                act.activation(spread[32:40, TP:T], spread[0:8, TP:T], ACT.Exp, bias=m0[:, 0:1]).then_inc(g_act, 1)

            @block.tensor
            def _(pe):
                pe.wait_ge(g_act, 6)
                for t, (t0, n) in enumerate(TILES):
                    mm = pe.transpose(aux[0][0:n, t * P:(t + 1) * P], turned_rows[:, t0:t0 + n], ident[:, :])
                mm.then_inc(g_pe, 1)
                for s in range(2):
                    mm = pe.transpose(aux[1][0:96, s * P:(s + 1) * P],
                                      conv_end[:, s, :, :].rearrange("p j m -> p (j m)"), ident[:, :])
                mm.then_inc(g_pe, 1)
                for h in range(HEADS):
                    mm = pe.matmul(aux[2][:, h * DEC:(h + 1) * DEC], pick[32:40, h, :], spread[32:40, TP:T],
                                   start=True, stop=True)
                mm.then_inc(g_pe, 1)
                for h in range(HEADS):
                    if h >= 4:
                        pe.wait_ge(g_cols, 3 + h - 3)
                    pe.matmul(acc[h % 4][:, 0:T], pick[0:8, h, :], spread[0:8, :], start=True,
                              stop=True).then_inc(g_pe, 1)

        p2 = ExitStack()
        k_in, v_in = sb("k_in", [P, 3, HD], F32, p2), sb("v_in", [P, 3, HD], F32, p2)
        k_new = sb("k_new", [TAIL, HD], F32, p2)
        skip_in = sb("skip_in", [P, HT, T], F32, p2)
        C_in = sb("C_in", [P, HT, HD], F32, p2)
        C_out = sb("C_out", [P, 2, HD], F32, p2)
        Dm, Pm = sb("Dm", [P, 528], F32, p2), sb("Pm", [P, 528], F32, p2)
        aq = sb("aq", [P, HT, TAIL], F32, p2)
        n0 = sb("n0", [P, HT], F32, p2)
        zs = sb("zs", [P, HT, T], F32, p2)
        hn = sb("hn", [P, 3, HD], F32, p2)
        hz_hi, hz_lo = sb("hz_hi", [P, HT, T], F32R, p2), sb("hz_lo", [P, HT, T], F32R, p2)
        st = sb("st", [P, 12, 3], F32, p2)
        stats = sb("stats", [P, 3, 6], F32, p2)
        mv = sb("mv", [P, 3, 2], F32, p2)
        n_out = sb("n_out", [64, P], F32, p2)
        p2.close()
        (kv_landed, C_landed, skip_landed, exp_in, exp_made, pairs_ready, z_made, kw_ready, den_ready,
         den_taken, n_ready, n_taken, var_ready, ln_made, exp_y, hn_ready, gated, hz_hi_made, hz_ready,
         head_set) = (sem("m_" + n) for n in (
             "kv_landed", "C_landed", "skip_landed", "exp_in", "exp_made", "pairs_ready", "z_made",
             "kw_ready", "den_ready", "den_taken", "n_ready", "n_taken", "var_ready", "ln_made", "exp_y",
             "hn_ready", "gated", "hz_hi_made", "hz_ready", "head_set"))
        b_ready = sem("m_ready")
        b_free = [sem(f"m_free{b}") for b in range(3)]
        pC_stored = [sem(f"pC_stored{b}") for b in range(2)]
        sC_stored, n_stored = sem("sC_stored"), sem("n_stored")
        USES = 15
        C_OUT = C_MIX + 16 * HEADS
        A_OUT = A_MIX + 20 * HEADS

        def kv_chunk_load(sp, n, g, j):
            col = g.times(HD) + (D * (j // 8) + CW * (j % 8 // 4))
            load_chunk(sp, n, i["w_kvf"][512 * (j % 4):512 * (j % 4 + 1), bass.ds(col.value, CW)])

        with nc.Block() as block:
            def steps(h, first, last=False):
                if first:
                    return [(Count(C_MIX + j), j, Count(A_MIX + 2 * (j // 4))) for j in range(8)]
                return [(h.times(16) + (C_MIX - 8 + j), j,
                         h.times(20) + (A_MIX - 16 + (2 * (j // 4) if j < 8 else 4 + 2 * (j - 8)))) for j in range(16)]

            last_steps = [(Count(C_OUT - 8 + j), 8 + j, Count(A_OUT - 16 + 2 * j)) for j in range(8)]

            def out_load(sp, n, h, j):
                w = i["a_w_out"][0, bass.ds(h.times(HD).value, HD), CW * j:CW * (j + 1)]
                load_chunk(sp, n, w)

            @block.sync
            def _(sp):
                for j in range(SLOTS, 8):
                    z_load(sp, Count(C_MIX + j), Count(0), j)

                with sp.Fori(0, HEADS - 1) as it:
                    h = Count(1, 1, it)
                    for n, j, _ in steps(h, False):
                        if j < 8:
                            z_load(sp, n, h, j)
                        else:
                            out_load(sp, n, h + -1, j - 8)
                for n, j, _ in last_steps:
                    out_load(sp, n, Count(HEADS - 1), j - 8)
                for j in range(SLOTS):
                    kv_chunk_load(sp, Count(C_OUT + j), Count(0), j)

            @block.gpsimd
            def _(pool):
                own = Own(pool, pool_own, counted["pool"])

                def kv_load(h):
                    for src, dst in ((k_dram, k_in), (v_dram, v_in)):
                        pool.dma_start(dst[:, 0:2, :], src[h.value, 0:256, :].rearrange("(t p) c -> p t c", p=P))\
                            .then_inc(kv_landed, 16)
                        pool.dma_start(dst[0:TAIL, 2, :], src[h.value, 256:T, :]).then_inc(kv_landed, 16)

                def C_load(h):
                    pool.dma_start(C_in[:, :, :], i["state_C"][0, 0, h.value].rearrange("(d p) e -> p d e", p=P))\
                        .then_inc(C_landed, 16)

                def skip_load(h):
                    pool.dma_start(skip_in[:, :, :], s_dram[h.value]).then_inc(skip_landed, 16)

                def turn(h, last=False):
                    for d in range(HT):
                        for k in (3 + 2 * d, 4 + 2 * d):
                            u = h.times(USES) + k
                            wait(pool, b_free[u.turn(3)], u.rounds(3) + 1)
                            settled(own, cell[:, :])
                            if k % 2:
                                pool.dma_start(o["p_C"][0, 0, h.value, d * P:(d + 1) * P, :], C_out[:, d % 2, :])\
                                    .then_inc(pC_stored[d % 2], 16)
                            else:
                                pool.dma_start(o["s_C"][0, 0, h.value, d * P:(d + 1) * P, :], C_in[:, d, :])\
                                    .then_inc(sC_stored, 16)
                    if not last:
                        kv_load(h + 1)
                        wait(pool, sC_stored, (h + 1).times(64))
                        settled(own, cell[:, :])
                        C_load(h + 1)
                        wait(pool, gated, (h + 1).times(HT))
                        settled(own, cell[:, :])
                        skip_load(h + 1)

                kv_load(Count(0))
                C_load(Count(0))
                skip_load(Count(0))
                turn(Count(0))
                with pool.Fori(0, HEADS - 2) as it:
                    own.open(it, 10)
                    turn(Count(1, 1, it))
                    own.close(HEADS - 2)
                turn(Count(HEADS - 1), last=True)
                wait(pool, sC_stored, HEADS * 64)
                wait(pool, pC_stored[0], HEADS * 32)
                wait(pool, pC_stored[1], HEADS * 32)
                pool.wait_ge(n_taken, HEADS + 1)
                for s, name in enumerate(("p_n", "s_n")):
                    pool.dma_start(o[name][0, 0].rearrange("h (d p) -> (h d) p", p=P), n_out[32 * s:32 * s + 32, :])\
                        .then_inc(n_stored, 16)
                pool.wait_ge(n_stored, 32)
                counted["pool"] = own.n

            @block.scalar
            def _(act):
                def exps(h):
                    wait(act, exp_in, h + 1)
                    for t, (c0, c1, n) in enumerate(((0, T, P), (T, 480, P), (480, 528, TAIL))):
                        ins = act.activation(Dm[0:n, c0:c1], Dm[0:n, c0:c1], ACT.Exp,
                                             bias=cols[0:n, t, bass.ds((h + U_COL).value, 1)])
                    ins.then_inc(exp_made, 1)

                def weight_keys(h):
                    wait(act, kv_landed, (h + 1).times(64))
                    wait(act, b_ready, h.times(USES))
                    act.activation(k_new[:, :], k_in[0:TAIL, 2, :], ACT.Copy,
                                   scale=cols[0:TAIL, 2, bass.ds((h + WS_COL).value, 1)]).then_inc(kw_ready, 1)
                    wait(act, kw_ready, h.times(2) + 1)
                    for t, (_, n) in enumerate(TILES):
                        ins = act.activation(k_in[0:n, t, :], k_in[0:n, t, :], ACT.Copy,
                                             scale=cols[0:n, t, bass.ds((h + WP_COL).value, 1)])
                    ins.then_inc(kw_ready, 1)

                def silu_z(tile):
                    for b in range(4):
                        wait(act, acc_free[b], (tile + -2).rounds(4) + 1)
                    act.activation(zs[:, :, :], zs[:, :, :], ACT.Silu).then_inc(z_made, 1)

                def inverse_norm(h):
                    wait(act, var_ready, h + 1)
                    act.activation(st[:, 5, :], st[:, 4, :], ACT.Ln).then_inc(ln_made, 1)
                    wait(act, ln_made, h + 1)
                    act.activation(st[:, 6, :], st[:, 5, :], ACT.Exp, scale=-0.5).then_inc(exp_y, 1)

                def take_state(h, d):
                    u = h.times(USES) + (3 + 2 * d)
                    wait(act, b_ready, u + 1)
                    wait(act, pC_stored[d % 2], h.times(32) + 16 * (d // 2))
                    act.activation(C_out[:, d % 2, :], aux[u.turn(3)][:, :], ACT.Copy).then_inc(b_free[u.turn(3)], 1)

                def high_hz(h, m):
                    wait(act, gated, h.times(HT) + (m + 1))
                    act.activation(hz_hi[:, m, :], zs[:, m, :], ACT.Copy).then_inc(hz_hi_made, 1)

                def turn(h, first=False):
                    for n, j, tile in steps(h, first):
                        high_part(act, n + 2)
                        if j < 4 and not first:
                            high_hz(h + -1, j)
                        if j == 4:
                            exps(h)
                            weight_keys(h)
                        if j == 7:
                            silu_z(tile)
                        if j == 8:
                            inverse_norm(h)
                        if j > 8 and j % 2:
                            take_state(h, (j - 9) // 2)
                    if first:
                        inverse_norm(h)
                        for d in range(HT):
                            take_state(h, d)

                turn(Count(0), first=True)
                with act.Fori(0, HEADS - 1) as it:
                    turn(Count(1, 1, it))
                for m in range(HT):
                    high_hz(Count(HEADS - 1), m)
                for n, _, _ in last_steps:
                    high_part(act, n + 2)

            @block.vector
            def _(dve):
                own = Own(dve, dve_own, counted["dve"])

                def step(ins):
                    own.done(ins)
                    own.wait()

                def exponents(h):
                    wait(dve, pairs_ready, h)
                    wait(dve, b_ready, h.times(USES))
                    for c0, c1, n, t0 in ((0, T, P, 0), (T, 480, P, P), (480, 528, TAIL, 256)):
                        ins = dve.tensor_tensor(Dm[0:n, c0:c1], negM[0:n, h.value, t0:T], mask[0:n, c0:c1], ALU.add)
                    ins.then_inc(exp_in, 1)
                    dve.tensor_tensor(aq[:, :, 16:TAIL], q_new[:, h.value, :, :],
                                      a_row[:, h.value, :].unsqueeze(1).to_broadcast([P, HT, DEC]), ALU.mult)
                    own.done(dve.tensor_copy(n0[:, :], par[:, bass.ds((h.times(HT) + N00).value, HT)]))

                def pairs(h):
                    wait(dve, exp_made, h + 1)
                    dve.tensor_tensor(Pm[:, 0:480], S_raw[:, h.value, 0:480], Dm[:, 0:480], ALU.mult)
                    dve.tensor_tensor(Pm[0:TAIL, 480:528], S_raw[0:TAIL, h.value, 480:528], Dm[0:TAIL, 480:528],
                                      ALU.mult).then_inc(pairs_ready, 1)

                def take_z(h, n, m0, tile):
                    if m0 == 0:
                        wait(dve, hz_ready, h.times(HT))
                    for m in (m0, m0 + 1):
                        u = tile + (m - m0)
                        wait(dve, used, n + 1)
                        dve.tensor_tensor(zs[:, m, :], acc[u.turn(4)][:, 0:T], rstd_row[:, :],
                                          ALU.mult).then_inc(acc_free[u.turn(4)], 1)

                def norm(h):
                    wait(dve, den_ready, h + 1)
                    dve.tensor_copy(st[:, 0, 0:2], aux[3][:, 0:2])
                    dve.tensor_copy(st[0:TAIL, 0, 2:3], aux[3][0:TAIL, 2:3]).then_inc(den_taken, 1)
                    wait(dve, den_taken, h + 1)
                    step(dve.scalar_tensor_tensor(st[:, 1, :], st[:, 0, :], -1.0, st[:, 0, :], ALU.mult, ALU.max))
                    step(dve.tensor_tensor(st[:, 1, :], st[:, 1, :],
                                           cols[:, :, bass.ds((h + EM_COL).value, 1)].rearrange("p t c -> p (t c)"),
                                           ALU.max))
                    own.done(dve.reciprocal(st[:, 2, :], st[:, 1, :]))
                    for t, (_, n) in enumerate(TILES):
                        u = h.times(USES) + t
                        own.done(dve.bn_stats(stats[0:n, t, :], aux[u.turn(3)][0:n, :]))
                    own.wait()
                    own.done(dve.tensor_tensor(st[:, 3, :], st[:, 2, :], st[:, 2, :], ALU.mult))
                    for t, (_, n) in enumerate(TILES):
                        own.done(dve.bn_aggr(mv[0:n, t, :], stats[0:n, t, :]))
                    own.wait()
                    step(dve.tensor_tensor(st[:, 3, :], st[:, 3, :], mv[:, :, 1:2].rearrange("p t c -> p (t c)"), ALU.mult))
                    dve.tensor_scalar(st[:, 4, :], st[:, 3, :], EPS, None, ALU.add).then_inc(var_ready, 1)
                    wait(dve, exp_y, h + 1)
                    newton(dve, own, st[:, 6, :], st[:, 4, :], st[:, 7, :])
                    step(dve.tensor_tensor(st[:, 8, :], st[:, 2, :], st[:, 6, :], ALU.mult))
                    for t, (_, n) in enumerate(TILES):
                        u = h.times(USES) + t
                        if t == 0:
                            wait(dve, b_ready, h.times(USES))
                        dve.tensor_scalar(hn[0:n, t, :], aux[u.turn(3)][0:n, :], mv[0:n, t, 0:1], st[0:n, 8, t:t + 1],
                                          ALU.subtract, ALU.mult).then_inc(b_free[u.turn(3)], 1)

                def take_state(h, d):
                    u = h.times(USES) + (4 + 2 * d)
                    wait(dve, b_ready, u + 1)
                    dve.scalar_tensor_tensor(C_in[:, d, :], C_in[:, d, :], a_row[:, h.value, DEC - 1:DEC],
                                             aux[u.turn(3)][:, :], ALU.mult, ALU.add).then_inc(b_free[u.turn(3)], 1)

                def take_n(h):
                    wait(dve, n_ready, h + 1)
                    dve.tensor_copy(n_all[:, 0, h.value, :], aux[3][:, 4:8])
                    dve.scalar_tensor_tensor(n_all[:, 1, h.value, :], n0[:, :], a_row[:, h.value, DEC - 1:DEC],
                                             aux[3][:, 8:12], ALU.mult, ALU.add).then_inc(n_taken, 1)

                def skip_and_gate(h, m):
                    u = h.times(USES) + (11 + m)
                    if m == 0:
                        wait(dve, skip_landed, (h + 1).times(16))
                        wait(dve, z_made, h + 1)
                    wait(dve, b_ready, u + 1)
                    g = par[:, bass.ds((h.times(HT) + (OUTG0 + m)).value, 1)]
                    dve.scalar_tensor_tensor(skip_in[:, m, :], aux[u.turn(3)][:, 0:T], g, skip_in[:, m, :],
                                             ALU.mult, ALU.add).then_inc(b_free[u.turn(3)], 1)
                    wait(dve, b_free[u.turn(3)], u.rounds(3) + 1)
                    dve.tensor_tensor(zs[:, m, :], zs[:, m, :], skip_in[:, m, :], ALU.mult).then_inc(gated, 1)

                def low_hz(h, m):
                    wait(dve, hz_hi_made, h.times(HT) + (m + 1))
                    dve.tensor_tensor(hz_lo[:, m, :], zs[:, m, :], hz_hi[:, m, :].bitcast(F32),
                                      ALU.subtract).then_inc(hz_ready, 1)

                def add_out(n, j, tile):
                    for m in range(2):
                        u = tile + m
                        wait(dve, used, n + 1)
                        x = xT[:, 2 * (j - 8) + m, :]
                        dve.tensor_tensor(x, x, acc[u.turn(4)][:, 0:T], ALU.add).then_inc(acc_free[u.turn(4)], 1)

                def turn(h, first=False):
                    for n, j, tile in steps(h, first):
                        low_part(dve, n + 2)
                        if j < 4 and not first:
                            low_hz(h + -1, j)
                        if j == 3:
                            take_z(h, n, 0, tile)
                        if j == 4:
                            exponents(h)
                        if j == 6:
                            pairs(h)
                        if j == 7:
                            take_z(h, n, 2, tile)
                        if j == 8:
                            norm(h)
                        if j >= 8:
                            add_out(n, j, tile)
                        if j > 8 and j % 2 == 0:
                            take_state(h, (j - 10) // 2)
                    if first:
                        norm(h)
                        for d in range(HT - 1):
                            take_state(h, d)
                    take_state(h, HT - 1)
                    take_n(h)
                    for m in range(HT):
                        skip_and_gate(h, m)

                dve.memset(st[:, :, :], 1.0).then_inc(head_set, 1)
                dve.memset(mv[:, :, :], 1.0).then_inc(head_set, 1)
                dve.memset(aq[:, :, 0:16], 0.0).then_inc(head_set, 1)
                dve.wait_ge(head_set, 3)
                turn(Count(0), first=True)
                with dve.Fori(0, HEADS - 1) as it:
                    own.open(it, M_OWN)
                    turn(Count(1, 1, it))
                    own.close(HEADS - 1)
                for m in range(HT):
                    low_hz(Count(HEADS - 1), m)
                dve.wait_ge(b_ready, USES * HEADS + 1)
                dve.tensor_copy(n_out[:, :], aux[0][0:64, 0:P]).then_inc(n_taken, 1)
                for n, j, tile in last_steps:
                    low_part(dve, n + 2)
                    add_out(n, j, tile)
                counted["dve"] = own.n

            @block.tensor
            def _(pe):
                def outputs(h):
                    wait(pe, pairs_ready, h + 1)
                    wait(pe, kv_landed, (h + 1).times(64))
                    wait(pe, C_landed, (h + 1).times(16))
                    wait(pe, n_taken, h)
                    for t, (_, n) in enumerate(TILES):
                        u = h.times(USES) + t
                        b = u.turn(3)
                        wait(pe, b_free[b], u.rounds(3))
                        parts = [(Pm[:, t * P:t * P + n], v_in[:, 0, :], ones[:, 0:1])]
                        if t > 0:
                            parts.append((Pm[:, T + (t - 1) * P:T + (t - 1) * P + n], v_in[:, 1, :], ones[:, 0:1]))
                        if t > 1:
                            parts.append((Pm[0:TAIL, 480:528], v_in[0:TAIL, 2, :], ones[0:TAIL, 0:1]))
                            parts += [(aq[:, d, :], C_in[:, d, :], n0[:, d:d + 1]) for d in range(HT)]
                        for k, (p_, v_, one) in enumerate(parts):
                            ends = dict(start=k == 0, stop=k == len(parts) - 1)
                            mm = pe.matmul(aux[b][0:n, :], p_, v_, **ends)
                        mm.then_inc(b_ready, 1)
                        for k, (p_, v_, one) in enumerate(parts):
                            ends = dict(start=k == 0, stop=k == len(parts) - 1)
                            mm = pe.matmul(aux[3][0:n, t:t + 1], p_, one, **ends)
                    mm.then_inc(den_ready, 1)

                def new_state(h, d, sample):
                    u = h.times(USES) + (3 + 2 * d + sample)
                    b = u.turn(3)
                    cut = slice(d * P, (d + 1) * P)
                    if d == 0 and not sample:
                        wait(pe, kw_ready, h.times(2) + 2)
                        wait(pe, den_taken, h + 1)
                    wait(pe, b_free[b], u.rounds(3))
                    parts = [(k_new[:, cut], v_in[0:TAIL, 2, :], ones[0:TAIL, 0:1])] if sample else \
                            [(k_in[0:n, t, cut], v_in[0:n, t, :], ones[0:n, 0:1]) for t, (_, n) in enumerate(TILES)]
                    col = 4 + 4 * sample + d
                    for k, (k_, _, one) in enumerate(parts):
                        mm = pe.matmul(aux[3][:, col:col + 1], k_, one, start=k == 0, stop=k == len(parts) - 1)
                    if d == HT - 1 and sample:
                        mm.then_inc(n_ready, 1)
                    for k, (k_, v_, _) in enumerate(parts):
                        mm = pe.matmul(aux[b][:, :], k_, v_, start=k == 0, stop=k == len(parts) - 1)
                    mm.then_inc(b_ready, 1)

                def turn_normed(h):
                    for m in range(HT):
                        u = h.times(USES) + (11 + m)
                        b = u.turn(3)
                        wait(pe, b_free[b], u.rounds(3))
                        for t, (t0, n) in enumerate(TILES):
                            mm = pe.transpose(aux[b][:, t0:t0 + n], hn[0:n, t, m * P:(m + 1) * P], ident[0:n, 0:n])
                        mm.then_inc(b_ready, 1)

                def turn(h, first=False):
                    for n, j, tile in steps(h, first):
                        if j == 8:
                            outputs(h)
                        if j < 8:
                            products(pe, n, tile, xg_hi, xg_lo, 4 * (j % 4), j % 4 == 0, j % 4 == 3)
                        else:
                            wait(pe, hz_ready, h.times(HT))
                            products(pe, n, tile, hz_hi, hz_lo, 0, True, True)
                            if j > 8:
                                new_state(h, (j - 9) // 2, (j - 9) % 2)
                    if first:
                        outputs(h)
                        for c in range(7):
                            new_state(h, c // 2, c % 2)
                    new_state(h, HT - 1, 1)
                    turn_normed(h)

                turn(Count(0), first=True)
                with pe.Fori(0, HEADS - 1) as it:
                    turn(Count(1, 1, it))
                pe.wait_ge(b_free[0], USES // 3 * HEADS)
                pe.wait_ge(n_taken, HEADS)
                pe.transpose(aux[0][0:64, 0:P], n_all[:, :, :, :].rearrange("p s h d -> p (s h d)"), ident[:, :])\
                    .then_inc(b_ready, 1)
                wait(pe, hz_ready, HEADS * HT)
                for n, j, tile in last_steps:
                    products(pe, n, tile, hz_hi, hz_lo, 0, True, True)

        ph.close()
        C_FOX = C_OUT + 16 * GROUPS
        A_FOX = A_OUT + 8 * GROUPS
        FP, FC, FN = 0, TP, TP + PAST
        pf = whole.enter_context(ExitStack())
        F_row = sb("F_row", [BH, TP + PAST + TAIL], F32, pf)
        rcol = sb("rcol", [P, 2, 3], F32, pf)
        tri = sb("tri", [P, P], mybir.dt.bfloat16, pf)
        tri_new = sb("tri_new", [DEC, TAIL], mybir.dt.bfloat16, pf)
        ident_bf = sb("ident_bf", [P, P], mybir.dt.bfloat16, pf)
        kT_dram = nc.dram_tensor("kT_scratch", (GROUPS, P, GRP, T), F32, kind="Internal").ap()
        v2_dram = nc.dram_tensor("v_fox_scratch", (T, D), F32, kind="Internal").ap()

        p3 = ExitStack()
        xk_hi, xk_lo = sb("xk_hi", [P, KD, T], F32R, p3), sb("xk_lo", [P, KD, T], F32R, p3)
        sq = sb("sq", [P, 2, T], F32, p3)
        ssum = sb("ssum", [P, T], F32, p3)
        ntmp = sb("ntmp", [P, 3, T], F32, p3)
        wf_in = sb("wf_in", [P, KD, BH], F32, p3)
        wf = sb("wf", [P, KD, P], F32R, p3)
        kf, vf = sb("kf", [P, GRP, T], F32, p3), sb("vf", [P, GRP, T], F32, p3)
        k_t, v_t = sb("k_t", [P, 3, HD], F32, p3), sb("v_t", [P, 3, HD], F32, p3)
        k_sq = sb("k_sq", [P, 3, HD], F32, p3)
        kb = sb("kb", [P, GRP, T], F32, p3)
        gk = sb("gk", [P, HD], F32, p3)
        kst = sb("kst", [P, 6, 3 * GRP], F32, p3)
        frow = {name: sb(f"f_{name}", [BH, T], F32, p3) for name in ("f", "abs", "e", "l", "lf", "sum", "low")}
        bf = sb("bf", [BH, 1], F32, p3)
        clf = sb("clf", [P, 4, BH], F32, p3)
        lf_out = sb("lf_out", [P, 3, BH], F32, p3)
        p3.close()
        (x_sq, x_sum, xk_hi_made, xk_lo_made, ss_made, v_made, n_ln, n_exp, norm_ready, f_in, f_hi, f_lo,
         f_done, f_dve, f_act, lf_turned, lf_taken, cols_turned, cols_taken, fox_set, fox_masks,
         k_squared, k_var, k_ln, k_exp, k_final, gk_landed, k_out, kT_out, v_out,
         lf_stored) = (sem("f_" + n) for n in (
             "x_sq", "x_sum", "xk_hi_made", "xk_lo_made", "ss_made", "v_made", "n_ln", "n_exp", "norm_ready",
             "in", "hi", "lo", "done", "dve", "act", "lf_turned", "lf_taken", "cols_turned", "cols_taken",
             "set", "masks", "k_squared", "k_var", "k_ln", "k_exp", "k_final",
             "gk_landed", "k_out", "kT_out", "v_out", "lf_stored"))
        t_ready, last_out = sem("t_ready"), sem("last_out")
        F_OWN = 10

        def fox_load(sp, n, g, j):
            if j < 16:
                col = g.times(HD) + (D * (j // 8) + CW * (j % 8 // 4))
                load_chunk(sp, n, i["b_w_in"][0, 512 * (j % 4):512 * (j % 4 + 1), bass.ds(col.value, CW)])
            else:
                row = (g + -1).times(HD)
                load_chunk(sp, n, i["b_w_out"][0, bass.ds(row.value, HD), CW * (j - 16):CW * (j - 15)])

        t_free = [sem(f"t_free{b}") for b in range(3)]

        def head_parts(ap, n):
            return ap.rearrange("p (h d) -> p h d", d=P)

        with nc.Block() as block:
            def steps(g):
                return [(g.times(16) + (C_OUT + j), j, g.times(8) + (A_OUT + 2 * (j // 4))) for j in range(16)]

            def by_head(name, t0, t1, g):
                return o[name][0, t0:t1, bass.ds(g.times(GRP).value, GRP), :]

            def store(eng, g, name, src, done):
                eng.dma_start(by_head("p_" + name, 0, 256, g).rearrange("(t p) h d -> p t h d", p=P),
                               src[:, 0:2, :].rearrange("p t (h d) -> p t h d", d=P)).then_inc(done, 16)
                eng.dma_start(by_head("p_" + name, 256, TP, g), head_parts(src[0:16, 2, :], 16)).then_inc(done, 16)
                eng.dma_start(by_head("s_" + name, 0, DEC, g), head_parts(src[16:TAIL, 2, :], DEC))\
                    .then_inc(done, 16)

            def store_values(eng, g, done):
                store(eng, g, "v", v_t, done)
                cols_ = bass.ds(g.times(HD).value, HD)
                eng.dma_start(v2_dram[0:256, cols_].rearrange("(t p) c -> p t c", p=P), v_t[:, 0:2, :])\
                   .then_inc(done, 16)
                eng.dma_start(v2_dram[256:T, cols_], v_t[0:TAIL, 2, :]).then_inc(done, 16)

            @block.sync
            def _(sp):
                for j in range(SLOTS, 16):
                    kv_chunk_load(sp, Count(C_OUT + j), Count(0), j)
                with sp.Fori(0, GROUPS - 1) as it:
                    g = Count(1, 1, it)
                    for n, j, _ in steps(g):
                        kv_chunk_load(sp, n, g, j)
                for j in range(SLOTS):
                    fox_load(sp, Count(C_FOX + j), Count(0), j)
                for b in range(3):
                    sp.wait_ge(t_free[b], 3 * GROUPS)
                store_values(sp, Count(GROUPS - 1), last_out)
                sp.wait_ge(last_out, 80)

            @block.gpsimd
            def _(pool):
                own = Own(pool, pool_own, counted["pool"])
                pool.dma_start(wf_in[:, :, :], i["w_kvf"][:, 2 * D:2 * D + BH].rearrange("(k p) c -> p k c", p=P))\
                    .then_inc(f_in, 16)
                pool.dma_start(bf[:, :], i["b_f"].rearrange("(p a) -> p a", a=1)).then_inc(f_in, 16)
                pool.dma_start(clf[:, :, :], i["cache_logf"][0].rearrange("(t p) h -> p t h", p=P)).then_inc(f_in, 16)

                def gk_load(g):
                    src = i["k_norm_g"][bass.ds(g.times(GRP).value, GRP), :].rearrange("h d -> (h d)")
                    pool.dma_start(gk[:, :], src.unsqueeze(0).to_broadcast([P, HD])).then_inc(gk_landed, 16)

                gk_load(Count(0))
                pool.memset(tri[:, :], 0.0).then_inc(fox_masks, 1)
                pool.memset(tri_new[:, :], 0.0).then_inc(fox_masks, 1)
                pool.wait_ge(fox_masks, 2)
                pool.affine_select(out=tri[:, :], in_=tri[:, :], compare_op=ALU.is_ge, fill=NEG, base=0,
                                   pattern=[[-1, P]], channel_multiplier=1).then_inc(fox_masks, 1)
                pool.affine_select(out=tri_new[:, :], in_=tri_new[:, :], compare_op=ALU.is_ge, fill=NEG, base=16,
                                   pattern=[[-1, TAIL]], channel_multiplier=1).then_inc(fox_masks, 1)
                pool.wait_ge(fox_masks, 4)
                pool.memset(tri_new[:, 0:16], NEG).then_inc(fox_masks, 1)

                def keys_out(g):
                    wait(pool, k_final, (g + 1).times(3))
                    settled(own, cell[:, :])
                    store(pool, g, "k", k_t, k_out)
                    for b in range(3):
                        wait(pool, t_free[b], g.times(3) + 2)
                    settled(own, cell[:, :])
                    pool.dma_start(kT_dram[g.value], kb[:, :, :]).then_inc(kT_out, 16)

                def values_out(g):
                    for b in range(3):
                        wait(pool, t_free[b], (g + 1).times(3))
                    settled(own, cell[:, :])
                    store_values(pool, g, v_out)

                pool.wait_ge(lf_taken, 1)
                for name, t0, t1, src in (("p", 0, P, lf_out[:, 0, :]), ("p", P, 256, lf_out[:, 1, :]),
                                          ("p", 256, TP, lf_out[0:16, 2, :]), ("s", 0, DEC, lf_out[16:TAIL, 2, :])):
                    pool.dma_start(o[name + "_logf"][0, t0:t1, :], src).then_inc(lf_stored, 16)
                keys_out(Count(0))
                with pool.Fori(0, GROUPS - 1) as it:
                    own.open(it, 4)
                    g = Count(1, 1, it)
                    wait(pool, k_final, g.times(3))
                    settled(own, cell[:, :])
                    gk_load(g)
                    values_out(g + -1)
                    keys_out(g)
                    own.close(GROUPS - 1)
                pool.wait_ge(lf_stored, 64)
                pool.wait_ge(k_out, 48 * GROUPS)
                pool.wait_ge(kT_out, 16 * GROUPS)
                pool.wait_ge(v_out, 80 * (GROUPS - 1))
                counted["pool"] = own.n

            @block.scalar
            def _(act):
                def take(dst, n, j, tile):
                    for m in range(2):
                        u = tile + m
                        wait(act, used, n + 1)
                        act.activation(dst[:, 2 * (j % 8 // 4) + m, :], acc[u.turn(4)][:, 0:T],
                                       ACT.Copy).then_inc(acc_free[u.turn(4)], 1)

                def keys_by_token(g):
                    wait(act, k_out, g.times(48))
                    act.wait_ge(cols_taken, 1)
                    for t, (_, n) in enumerate(TILES):
                        u = g.times(9) + t
                        wait(act, t_ready, u + 1)
                        act.activation(k_t[0:n, t, :], aux[u.turn(3)][0:n, :], ACT.Copy,
                                       scale=rcol[0:n, 0, t:t + 1]).then_inc(t_free[u.turn(3)], 1)
                        wait(act, t_free[u.turn(3)], u.rounds(3) + 1)
                        act.activation(k_sq[0:n, t, :], k_t[0:n, t, :], ACT.Square).then_inc(k_squared, 1)

                def inverse_norms(g):
                    wait(act, k_var, g + 1)
                    act.activation(kst[:, 2, :], kst[:, 1, :], ACT.Ln).then_inc(k_ln, 1)
                    wait(act, k_ln, g + 1)
                    act.activation(kst[:, 3, :], kst[:, 2, :], ACT.Exp, scale=-0.5).then_inc(k_exp, 1)

                def values_by_token(g):
                    wait(act, v_out, g.times(80))
                    for t, (_, n) in enumerate(TILES):
                        u = g.times(9) + (6 + t)
                        wait(act, t_ready, u + 1)
                        act.activation(v_t[0:n, t, :], aux[u.turn(3)][0:n, :], ACT.Copy,
                                       scale=rcol[0:n, 0, t:t + 1]).then_inc(t_free[u.turn(3)], 1)
                        wait(act, t_free[u.turn(3)], u.rounds(3) + 1)

                def turn(g, first=False):
                    for n, j, tile in steps(g):
                        high_part(act, n + 2)
                        if first and j < 4:
                            squares(4 * j)
                        if first and j == 5:
                            inverse_rms()
                        if first and j == 9:
                            forget_2()
                        if j in (3, 7):
                            if j == 3:
                                wait(act, t_ready, g.times(9) + (-6))
                            take(kf, n, j, tile)
                        if j in (11, 15):
                            take(vf, n, j, tile)
                        if j == 3 and not first:
                            values_by_token(g + -1)
                        if j == 9:
                            keys_by_token(g)
                        if j == 12:
                            inverse_norms(g)

                def inverse_rms():
                    act.wait_ge(v_made, 1)
                    act.activation(ntmp[:, 1, :], ntmp[:, 0, :], ACT.Ln).then_inc(n_ln, 1)
                    act.wait_ge(n_ln, 1)
                    act.activation(rstd_row[:, :], ntmp[:, 1, :], ACT.Exp, scale=-0.5).then_inc(n_exp, 1)

                def forget_2():
                    act.wait_ge(f_dve, 1)
                    act.activation(frow["e"][:, :], frow["abs"][:, :], ACT.Exp, scale=-1.0).then_inc(f_act, 1)
                    act.wait_ge(f_act, 1)
                    act.activation(frow["l"][:, :], frow["e"][:, :], ACT.Ln, bias=1.0).then_inc(f_act, 1)

                def squares(k0):
                    for k in range(k0, k0 + 4):
                        if k >= 2:
                            act.wait_ge(x_sum, k - 1)
                        act.activation(sq[:, k % 2, :], xT[:, k, :], ACT.Square).then_inc(x_sq, 1)

                for k in range(KD):
                    act.activation(xk_hi[:, k, :], xT[:, k, :], ACT.Copy,
                                   scale=par[:, GKV0 + k:GKV0 + k + 1]).then_inc(xk_hi_made, 1)
                act.wait_ge(f_in, 48)
                act.wait_ge(fox_set, 1)
                act.activation(wf[:, :, 0:BH], wf_in[:, :, :], ACT.Copy).then_inc(f_hi, 1)
                turn(Count(0), first=True)
                with act.Fori(0, GROUPS - 1) as it:
                    turn(Count(1, 1, it))
                values_by_token(Count(GROUPS - 1))

            @block.vector
            def _(dve):
                own = Own(dve, dve_own, counted["dve"])

                def step(ins):
                    own.done(ins)
                    own.wait()

                def norm_terms(g):
                    for t, (_, n) in enumerate(TILES):
                        wait(dve, k_squared, g.times(3) + (t + 1))
                        own.done(dve.tensor_reduce(kst[0:n, 0, GRP * t:GRP * (t + 1)], head_parts(k_sq[0:n, t, :], n),
                                                   AX.X, ALU.add))
                    own.wait()
                    dve.tensor_scalar(kst[:, 1, :], kst[:, 0, :], 1.0 / P, EPS, ALU.mult, ALU.add).then_inc(k_var, 1)

                def keys_final(g):
                    wait(dve, k_exp, g + 1)
                    newton(dve, own, kst[:, 3, :], kst[:, 1, :], kst[:, 4, :])
                    wait(dve, gk_landed, (g + 1).times(16))
                    for t, (_, n) in enumerate(TILES):
                        y = kst[0:n, 3, GRP * t:GRP * (t + 1)].unsqueeze(2).to_broadcast([n, GRP, P])
                        own.done(dve.tensor_tensor(head_parts(k_t[0:n, t, :], n), head_parts(k_t[0:n, t, :], n), y, ALU.mult))
                    own.wait()
                    for t, (_, n) in enumerate(TILES):
                        dve.tensor_tensor(k_t[0:n, t, :], k_t[0:n, t, :], gk[0:n, :], ALU.mult).then_inc(k_final, 1)

                def keys_back(g):
                    wait(dve, kT_out, g.times(16))
                    for t, (t0, n) in enumerate(TILES):
                        u = g.times(9) + (3 + t)
                        wait(dve, t_ready, u + 1)
                        dve.tensor_copy(kb[:, :, t0:t0 + n],
                                        aux[u.turn(3)][:, 0:GRP * n].rearrange("p (h n) -> p h n", n=n))\
                           .then_inc(t_free[u.turn(3)], 1)

                def turn(g, first=False):
                    for n, j, tile in steps(g):
                        low_part(dve, n + 2)
                        if first and j < 4:
                            sums(4 * j)
                        if first and j == 5:
                            norm_1()
                        if first and j == 6:
                            columns()
                        if first and j == 8:
                            forget_1()
                        if first and j == 10:
                            forget_2()
                        if j == 11:
                            norm_terms(g)
                        if first and j == 14:
                            forget_3()
                        if j == 13:
                            keys_final(g)
                        if j == 15:
                            keys_back(g)

                def sums(k0):
                    for k in range(k0, k0 + 4):
                        dve.wait_ge(x_sq, k + 1)
                        if k:
                            dve.wait_ge(x_sum, k)
                        dve.tensor_tensor(ssum[:, :], ssum[:, :], sq[:, k % 2, :], ALU.add).then_inc(x_sum, 1)

                def norm_1():
                    dve.wait_ge(ss_made, 1)
                    dve.tensor_scalar(ntmp[:, 0, :], aux[3][:, 0:T], 1.0 / D, EPS, ALU.mult, ALU.add).then_inc(v_made, 1)
                    dve.wait_ge(n_exp, 1)
                    newton(dve, own, rstd_row[:, :], ntmp[:, 0, :], ntmp[:, 2, :])
                    own.eng.tensor_copy(ntmp[:, 1, 0:1], rstd_row[:, 0:1]).then_inc(norm_ready, 1)

                def columns():
                    dve.wait_ge(cols_turned, 1)
                    for t, (_, n) in enumerate(TILES):
                        dve.tensor_copy(rcol[0:n, 0, t:t + 1], aux[3][0:n, t:t + 1])
                    for t, (_, n) in enumerate(QT):
                        ins = dve.tensor_copy(rcol[0:n, 1, t:t + 1], aux[3][0:n, 4 + t:5 + t])
                    ins.then_inc(cols_taken, 1)

                def forget_1():
                    dve.wait_ge(f_done, 1)
                    r = {k: v[:, :] for k, v in frow.items()}
                    step(dve.tensor_copy(r["low"], aux[3][32:32 + BH, 0:T]))
                    step(dve.tensor_tensor(r["sum"], r["low"], aux[3][0:BH, 0:T], ALU.add))
                    step(dve.tensor_tensor(r["sum"], r["sum"], rstd_row[0:BH, :], ALU.mult))
                    step(dve.tensor_scalar(r["f"], r["sum"], bf[:, 0:1], None, ALU.add))
                    dve.scalar_tensor_tensor(r["abs"], r["f"], -1.0, r["f"], ALU.mult, ALU.max).then_inc(f_dve, 1)

                def forget_2():
                    dve.wait_ge(f_act, 2)
                    r = {k: v[:, :] for k, v in frow.items()}
                    dve.scalar_tensor_tensor(r["lf"], r["f"], 0.0, r["l"], ALU.min, ALU.subtract).then_inc(f_dve, 1)
                    dve.wait_ge(f_dve, 2)

                    def one(n):
                        return ones[0:BH, 0:1].to_broadcast([BH, n])

                    step(dve.memset(F_row[:, FN:FN + 16], 0.0))
                    step(dve.tensor_tensor_scan(F_row[:, FP:FP + TP], one(TP), frow["lf"][:, 0:TP], 0.0,
                                                ALU.mult, ALU.add))
                    dve.wait_ge(cols_turned, 2)
                    step(dve.tensor_tensor_scan(F_row[:, FC:FC + PAST], one(PAST), aux[3][0:BH, 0:PAST], 0.0,
                                                ALU.mult, ALU.add))
                    dve.tensor_tensor_scan(F_row[:, FN + 16:FN + TAIL], one(DEC), frow["lf"][:, TP:T],
                                           F_row[:, FN - 1:FN], ALU.mult, ALU.add).then_inc(f_dve, 1)

                def forget_3():
                    dve.wait_ge(lf_turned, 1)
                    dve.tensor_copy(lf_out[:, 0:2, :], aux[3][:, 0:2 * BH].rearrange("p (t h) -> p t h", h=BH))
                    dve.tensor_copy(lf_out[0:TAIL, 2, :], aux[3][0:TAIL, 2 * BH:3 * BH]).then_inc(lf_taken, 1)

                for k in range(KD):
                    dve.wait_ge(xk_hi_made, k + 1)
                    dve.scalar_tensor_tensor(xk_lo[:, k, :], xT[:, k, :], par[:, GKV0 + k:GKV0 + k + 1],
                                             xk_hi[:, k, :].bitcast(F32), ALU.mult, ALU.subtract).then_inc(xk_lo_made, 1)
                dve.memset(wf[:, :, :].bitcast(F32), 0.0).then_inc(fox_set, 1)
                own.done(dve.memset(kst[:, :, :], 1.0))
                own.done(dve.tensor_copy(ident_bf[:, :], ident[:, :]))
                own.done(dve.memset(rcol[:, :, :], 1.0))
                own.done(dve.memset(ssum[:, :], 0.0))
                own.wait()
                dve.wait_ge(f_hi, 1)
                dve.tensor_tensor(wf[:, :, 32:32 + BH], wf_in[:, :, :], wf[:, :, 0:BH].bitcast(F32),
                                  ALU.subtract).then_inc(f_lo, 1)
                turn(Count(0), first=True)
                with dve.Fori(0, GROUPS - 1) as it:
                    own.open(it, F_OWN)
                    turn(Count(1, 1, it))
                    own.close(GROUPS - 1)
                counted["dve"] = own.n

            @block.tensor
            def _(pe):
                def banks_free(u):
                    for b in range(3):
                        wait(pe, t_free[b], u.rounds(3))

                def by_token(src, g, k):
                    banks_free(g.times(9) + k)
                    for t, (t0, n) in enumerate(TILES):
                        b = (g.times(9) + (k + t)).turn(3)
                        for m in range(GRP):
                            mm = pe.transpose(aux[b][0:n, m * P:(m + 1) * P], src[:, m, t0:t0 + n], ident[:, :])
                        mm.then_inc(t_ready, 1)

                def keys_back(g):
                    wait(pe, k_final, (g + 1).times(3))
                    banks_free(g.times(9) + 3)
                    for t, (t0, n) in enumerate(TILES):
                        b = (g.times(9) + (3 + t)).turn(3)
                        for m in range(GRP):
                            mm = pe.transpose(aux[b][:, m * n:(m + 1) * n], k_t[0:n, t, m * P:(m + 1) * P],
                                              ident[0:n, 0:n])
                        mm.then_inc(t_ready, 1)

                def taken_all(tile):
                    for b in range(4):
                        wait(pe, acc_free[b], tile.rounds(4) + 1)

                def turn(g, first=False):
                    for n, j, tile in steps(g):
                        if first and j < 4:
                            pe.wait_ge(xk_lo_made, 4 * (j + 1))
                        products(pe, n, tile, xk_hi, xk_lo, 4 * (j % 4), j % 4 == 0, j % 4 == 3)
                        if first:
                            extras(j)
                        if j == 2 and not first:
                            taken_all(tile + -4)
                            by_token(vf, g + -1, 6)
                        if j == 9:
                            taken_all(tile + -4)
                            by_token(kf, g, 0)
                        if j == 15:
                            keys_back(g)

                def extras(j):
                    if j == 4:
                        pe.wait_ge(x_sum, KD)
                        pe.matmul(aux[3][:, 0:T], ones[:, :], ssum[:, :], start=True, stop=True).then_inc(ss_made, 1)
                    if j == 5:
                        pe.wait_ge(norm_ready, 1)
                        for c, tiles in ((0, TILES), (4, [(t0 + META, n) for t0, n in QT])):
                            for t, (t0, n) in enumerate(tiles):
                                mm = pe.matmul(aux[3][0:n, c + t:c + t + 1], rstd_row[:, t0:t0 + n], ident[:, 0:1],
                                               start=True, stop=True)
                        mm.then_inc(cols_turned, 1)
                    if j == 7:
                        pe.wait_ge(cols_taken, 1)
                        pe.wait_ge(f_lo, 1)
                        for k in range(KD):
                            for part, x in enumerate((xk_hi, xk_lo)):
                                mm = pe.matmul(aux[3][:, 0:T], wf[:, k, :], x[:, k, :], start=k == 0 and part == 0,
                                               stop=k == KD - 1 and part == 1)
                        mm.then_inc(f_done, 1)
                    if j == 9:
                        pe.wait_ge(f_dve, 1)
                        pe.wait_ge(f_in, 48)
                        for t in range(4):
                            mm = pe.transpose(aux[3][0:BH, t * P:(t + 1) * P], clf[:, t, :], ident[:, :])
                        mm.then_inc(cols_turned, 1)
                    if j == 13:
                        pe.wait_ge(f_dve, 3)
                        for t, (t0, n) in enumerate(TILES):
                            mm = pe.transpose(aux[3][0:n, t * BH:(t + 1) * BH], frow["lf"][:, t0:t0 + n],
                                              ident[0:BH, 0:BH])
                        mm.then_inc(lf_turned, 1)

                turn(Count(0), first=True)
                with pe.Fori(0, GROUPS - 1) as it:
                    turn(Count(1, 1, it))
                taken_all(Count(A_FOX - 4))
                by_token(vf, Count(GROUPS - 1), 6)

        p4 = ExitStack()
        xb_hi, xb_lo = sb("xb_hi", [P, KD, TQ], F32R, p4), sb("xb_lo", [P, KD, TQ], F32R, p4)
        Kc, Vc = sb("Kc", [P, 4, HD], F32, p4), sb("Vc", [P, 4, HD], F32, p4)
        kT_in = sb("kT_in", [P, GRP, T], F32, p4)
        v_all = sb("v_all", [P, 3, HD], F32, p4)
        KcT = sb("KcT", [P, PAST], F32, p4)
        F2 = sb("F2", [48, TP + PAST + TAIL], F32R, p4)
        minus = sb("minus", [48, BH], F32, p4)
        sel = sb("sel", [48, GRP, P], F32R, p4)
        qf = sb("qf", [P, GRP, TQ], F32, p4)
        q_t, q_sq = sb("q_t", [P, 3, HD], F32, p4), sb("q_sq", [P, 3, HD], F32, p4)
        gq = sb("gq", [P, HD], F32, p4)
        qT = sb("qT", [P, GRP, TQ], F32, p4)
        qst = sb("qst", [P, 6, 3 * GRP], F32, p4)
        WA, WB, WZ = META + P, TP, TAIL
        CA, CB, CZ, CY = 0, WA, WA + WB, WA + WB + WZ
        Pf = sb("Pf", [P, CY + PAST], F32, p4)
        mx, nm, sm, rc = (sb(n, [P, 4], F32, p4) for n in ("mx", "nm", "sm", "rc"))
        PT, PT2 = sb("PT", [P, 512], F32, p4), sb("PT2", [TAIL, TQ], F32, p4)
        zg = sb("zg", [P, GRP, TQ], F32, p4)
        oz_hi, oz_lo = sb("oz_hi", [P, GRP, TQ], F32R, p4), sb("oz_lo", [P, GRP, TQ], F32R, p4)
        p4.close()
        (xb_hi_made, xb_lo_made, F_high, f_set, sel_made, kc_landed, kt_landed, v_landed, gq_landed,
         q_squared, q_var, q_ln, q_exp, q_final, max_ready, exp_done, probs_ready, zg_made, oz_hi_made,
         oz_ready, use_ready) = (sem("a_" + n) for n in (
             "xb_hi_made", "xb_lo_made", "F_high", "set", "sel_made", "kc_landed", "kt_landed",
             "v_landed", "gq_landed", "q_squared", "q_var", "q_ln", "q_exp", "q_final", "max_ready", "exp_done",
             "probs_ready", "zg_made", "oz_hi_made", "oz_ready", "use_ready"))
        use_free = [sem(f"use_free{b}") for b in range(4)]
        FOX_OWN = 3 + 4 + 1 + 3 + GRP * 7
        C_END = C_FOX + 24 * GROUPS
        BESIDE = {8: ["q"], 9: ["r"], 10: ["n"], 11: ["f"], 12: ["K0"], 13: ["b"], 14: ["S0"], 15: ["E0", "K1"],
                  16: ["N0", "z"], 17: ["T0", "S1"], 18: ["E1", "O0", "K2"], 19: ["N1"], 20: ["T1", "S2"],
                  21: ["E2", "O1", "K3"], 22: ["N2"], 23: ["T2", "S3"]}
        BESIDE_LAST = {0: ["E3", "O2"], 1: ["N3"], 2: ["T3"], 3: ["O3"]}
        USE, at = {}, 0
        for events in list(BESIDE.values()) + list(BESIDE_LAST.values()):
            for e in events:
                USE[e] = at
                at += {"q": 3, "b": 5, "K": 1, "S": 2, "T": 2, "O": 1}.get(e[0], 0)
        FOX_USES = at
        assert FOX_USES % 4 == 0
        BACK = [(0, 0, 2), (2, 0, GRP), (0, 2, GRP), (1, 0, 2), (1, 2, GRP)]

        with nc.Block() as block:
            def steps(g, first=False):
                if first:
                    return [(Count(C_FOX + j), j, Count(A_FOX + 2 * (j // 4))) for j in range(16)]
                return [(g.times(24) + (C_FOX - 8 + j), j,
                         g.times(24) + (A_FOX - 16 + (2 * (j // 4) if j < 16 else 8 + 2 * (j - 16)))) for j in range(24)]

            last_steps = [(Count(C_END - 8 + j), 16 + j, Count(A_FOX + 24 * GROUPS - 16 + 2 * j)) for j in range(8)]

            def use(g, e, k=0):
                return g.times(FOX_USES) + (USE[e] + k)

            def turns(g, first, chunk, event):
                for n, j, tile in steps(g, first):
                    chunk(g, n, j, tile)
                    if not first:
                        for e in BESIDE_LAST.get(j, []):
                            event(g + -1, e)
                    for e in BESIDE.get(j, []):
                        event(g, e)
                if first:
                    for j in range(16, 24):
                        for e in BESIDE[j]:
                            event(g, e)

            @block.sync
            def _(sp):
                for j in range(SLOTS, 16):
                    fox_load(sp, Count(C_FOX + j), Count(0), j)
                with sp.Fori(0, GROUPS - 1) as it:
                    g = Count(1, 1, it)
                    for n, j, _ in steps(g):
                        fox_load(sp, n, g, j)
                for n, j, _ in last_steps:
                    fox_load(sp, n, Count(GROUPS), j)

            @block.gpsimd
            def _(pool):
                own = Own(pool, pool_own, counted["pool"])

                def heads(g):
                    return bass.ds(g.times(HD).value, HD)

                def kc_load(g):
                    pool.dma_start(Kc[:, :, :], i["cache_k"][0].rearrange("(t p) h d -> p t (h d)", p=P)[:, :, heads(g)])\
                        .then_inc(kc_landed, 16)
                    src = i["q_norm_g"][0].rearrange("h d -> (h d)")[heads(g)]
                    pool.dma_start(gq[:, :], src.unsqueeze(0).to_broadcast([P, HD])).then_inc(gq_landed, 16)

                def kt_load(g):
                    pool.dma_start(kT_in[:, :, :], kT_dram[g.value]).then_inc(kt_landed, 16)

                def v_load(g):
                    pool.dma_start(Vc[:, :, :], i["cache_v"][0].rearrange("(t p) h d -> p t (h d)", p=P)[:, :, heads(g)])\
                        .then_inc(v_landed, 16)
                    pool.dma_start(v_all[:, 0:2, :], v2_dram[0:256, heads(g)].rearrange("(t p) c -> p t c", p=P))\
                        .then_inc(v_landed, 16)
                    pool.dma_start(v_all[0:TAIL, 2, :], v2_dram[256:T, heads(g)]).then_inc(v_landed, 16)

                def next_loads(g):
                    last = g + -1
                    wait(pool, use_ready, use(last, "K3") + 1)
                    settled(own, cell[:, :])
                    kc_load(g)
                    wait(pool, use_ready, use(last, "S3", 1) + 1)
                    settled(own, cell[:, :])
                    kt_load(g)
                    wait(pool, use_ready, use(last, "O3") + 1)
                    settled(own, cell[:, :])
                    v_load(g)

                kc_load(Count(0))
                kt_load(Count(0))
                v_load(Count(0))
                with pool.Fori(0, GROUPS - 1) as it:
                    own.open(it, 3)
                    next_loads(Count(1, 1, it))
                    own.close(GROUPS - 1)
                counted["pool"] = own.n

            @block.scalar
            def _(act):
                def take_q(g, n, j, tile):
                    wait(act, use_ready, use(g + -1, "q", 2) + 1)
                    for m in range(2):
                        u = tile + m
                        wait(act, used, n + 1)
                        act.activation(qf[:, 2 * (j // 4) + m, :], acc[u.turn(4)][:, 0:TQ],
                                       ACT.Copy).then_inc(acc_free[u.turn(4)], 1)

                def q_by_token(g):
                    for t, (_, n) in enumerate(QT):
                        u = use(g, "q", t)
                        wait(act, use_ready, u + 1)
                        act.activation(q_t[0:n, t, :], aux[u.turn(4)][0:n, :], ACT.Copy,
                                       scale=rcol[0:n, 1, t:t + 1]).then_inc(use_free[u.turn(4)], 1)
                        wait(act, use_free[u.turn(4)], u.rounds(4) + 1)
                        act.activation(q_sq[0:n, t, :], q_t[0:n, t, :], ACT.Square).then_inc(q_squared, 1)

                def inverse_norms(g):
                    wait(act, q_var, g + 1)
                    act.activation(qst[:, 2, :], qst[:, 1, :], ACT.Ln).then_inc(q_ln, 1)
                    wait(act, q_ln, g + 1)
                    act.activation(qst[:, 3, :], qst[:, 2, :], ACT.Exp, scale=-0.5).then_inc(q_exp, 1)

                def take_keys(g, e):
                    u = use(g, e)
                    wait(act, use_ready, u + 1)
                    act.activation(KcT[:, :], aux[u.turn(4)][:, :], ACT.Copy).then_inc(use_free[u.turn(4)], 1)

                def exps(g, e):
                    x = int(e[1])
                    u = use(g, e)
                    wait(act, max_ready, g.times(GRP) + (x + 1))
                    ab, y = aux[u.turn(4)], aux[(u + 1).turn(4)]
                    act.activation(Pf[:, CA:CA + WA], ab[:, CA:CA + WA], ACT.Exp, bias=nm[:, 0:1], accum_out=sm[:, 0:1])
                    act.activation(Pf[:, CB:CB + WB], ab[:, CB:CB + WB], ACT.Exp, bias=nm[:, 1:2], accum_out=sm[:, 1:2])
                    act.activation(Pf[0:DEC, CZ:CZ + WZ], ab[0:DEC, CZ:CZ + WZ], ACT.Exp, bias=nm[0:DEC, 2:3],
                                   accum_out=sm[0:DEC, 2:3]).then_inc(use_free[u.turn(4)], 1)
                    act.activation(Pf[0:DEC, CY:CY + PAST], y[0:DEC, 0:PAST], ACT.Exp, bias=nm[0:DEC, 2:3],
                                   accum_out=sm[0:DEC, 3:4]).then_inc(use_free[(u + 1).turn(4)], 1)

                def take_probs(g, e):
                    u = use(g, e)
                    wait(act, use_ready, u + 2)
                    b1, b2 = u.turn(4), (u + 1).turn(4)
                    act.activation(PT[:, :], aux[b1][:, :], ACT.Copy).then_inc(use_free[b1], 1)
                    act.activation(PT2[0:META, 0:256], aux[b2][0:META, 0:256], ACT.Copy)
                    act.activation(PT2[:, 256:TQ], aux[b2][0:TAIL, 256:TQ], ACT.Copy).then_inc(use_free[b2], 1)

                def silu_z(g):
                    z_tile = steps(g, not (g.a or g.b))[12][2]
                    for b in range(4):
                        wait(act, acc_free[b], z_tile.rounds(4) + 1)
                    act.activation(zg[:, :, :], zg[:, :, :], ACT.Silu).then_inc(zg_made, 1)

                def high_oz(g, m):
                    u = use(g, f"O{m}")
                    wait(act, use_free[u.turn(4)], u.rounds(4) + 1)
                    act.activation(oz_hi[:, m, :], zg[:, m, :], ACT.Copy).then_inc(oz_hi_made, 1)

                def event(g, e):
                    if e == "q":
                        q_by_token(g)
                    elif e == "n":
                        inverse_norms(g)
                    elif e[0] == "K":
                        take_keys(g, e)
                    elif e == "z":
                        silu_z(g)
                    elif e[0] == "E":
                        exps(g, "S" + e[1])
                    elif e[0] == "T":
                        take_probs(g, e)

                def chunk(g, n, j, tile):
                    high_part(act, n + 2)
                    if 4 <= j < 8 and (g.a or g.b):
                        high_oz(g + -1, j - 4)
                    if j in (3, 7):
                        take_q(g, n, j, tile)

                for k in range(KD):
                    act.activation(xb_hi[:, k, :], xT[:, k, META:T], ACT.Copy,
                                   scale=par[:, GB0 + k:GB0 + k + 1]).then_inc(xb_hi_made, 1)
                act.wait_ge(f_set, 1)
                act.activation(F2[0:BH, :], F_row[:, :], ACT.Copy).then_inc(F_high, 1)
                turns(Count(0), True, chunk, event)
                with act.Fori(0, GROUPS - 1) as it:
                    turns(Count(1, 1, it), False, chunk, event)
                last = Count(GROUPS - 1)
                for e in ("E3", "T3"):
                    event(last, e)
                for m in range(GRP):
                    high_oz(last, m)
                for n, _, _ in last_steps:
                    if n.a + 2 < C_END:
                        high_part(act, n + 2)

            @block.vector
            def _(dve):
                own = Own(dve, dve_own, counted["dve"])

                def step(ins):
                    own.done(ins)
                    own.wait()

                def q_terms(g):
                    for t, (_, n) in enumerate(QT):
                        wait(dve, q_squared, g.times(3) + (t + 1))
                        own.done(dve.tensor_reduce(qst[0:n, 0, GRP * t:GRP * (t + 1)], head_parts(q_sq[0:n, t, :], n),
                                                   AX.X, ALU.add))
                    own.wait()
                    dve.tensor_scalar(qst[:, 1, :], qst[:, 0, :], 1.0 / P, EPS, ALU.mult, ALU.add).then_inc(q_var, 1)
                    wait(dve, use_ready, use(g, "q") + 1)
                    dve.tensor_copy(sel[:, :, :], minus[:, bass.ds(g.times(GRP).value, GRP)].unsqueeze(2)
                                    .to_broadcast([48, GRP, P])).then_inc(sel_made, 1)

                def q_finals(g):
                    wait(dve, q_exp, g + 1)
                    newton(dve, own, qst[:, 3, :], qst[:, 1, :], qst[:, 4, :])
                    step(dve.tensor_scalar(qst[:, 3, :], qst[:, 3, :], P ** -0.5, None, ALU.mult))
                    wait(dve, gq_landed, (g + 1).times(16))
                    for t, (_, n) in enumerate(QT):
                        y = qst[0:n, 3, GRP * t:GRP * (t + 1)].unsqueeze(2).to_broadcast([n, GRP, P])
                        own.done(dve.tensor_tensor(head_parts(q_t[0:n, t, :], n), head_parts(q_t[0:n, t, :], n), y, ALU.mult))
                    own.wait()
                    for t, (_, n) in enumerate(QT):
                        dve.tensor_tensor(q_t[0:n, t, :], q_t[0:n, t, :], gq[0:n, :], ALU.mult).then_inc(q_final, 1)

                def q_back(g):
                    for k, (t, m0, m1) in enumerate(BACK):
                        t0, n = QT[t]
                        u = use(g, "b", k)
                        wait(dve, use_ready, u + 1)
                        dve.tensor_copy(qT[:, m0:m1, t0:t0 + n],
                                        aux[u.turn(4)][:, 0:(m1 - m0) * n].rearrange("p (h n) -> p h n", n=n))\
                           .then_inc(use_free[u.turn(4)], 1)

                def maxima(g, e):
                    u = use(g, e)
                    wait(dve, use_ready, u + 2)
                    ab, y = aux[u.turn(4)], aux[(u + 1).turn(4)]
                    own.done(dve.tensor_reduce(mx[:, 0:1], ab[:, CA:CA + WA], AX.X, ALU.max))
                    own.done(dve.tensor_reduce(mx[:, 1:2], ab[:, CB:CB + WB], AX.X, ALU.max))
                    own.done(dve.tensor_reduce(mx[0:DEC, 2:3], ab[0:DEC, CZ:CZ + WZ], AX.X, ALU.max))
                    own.done(dve.tensor_reduce(mx[0:DEC, 3:4], y[0:DEC, 0:PAST], AX.X, ALU.max))
                    own.wait()
                    step(dve.tensor_tensor(mx[0:DEC, 2:3], mx[0:DEC, 2:3], mx[0:DEC, 3:4], ALU.max))
                    dve.tensor_scalar(nm[:, :], mx[:, :], -1.0, None, ALU.mult).then_inc(max_ready, 1)

                def softmax(g, e):
                    u = use(g, "S" + e[1], 1)
                    wait(dve, use_free[u.turn(4)], u.rounds(4) + 1)
                    step(dve.tensor_tensor(sm[0:DEC, 2:3], sm[0:DEC, 2:3], sm[0:DEC, 3:4], ALU.add))
                    step(dve.reciprocal(rc[:, :], sm[:, :]))
                    dve.tensor_scalar(Pf[:, CA:CA + WA], Pf[:, CA:CA + WA], rc[:, 0:1], None, ALU.mult)
                    dve.tensor_scalar(Pf[:, CB:CB + WB], Pf[:, CB:CB + WB], rc[:, 1:2], None, ALU.mult)
                    dve.tensor_scalar(Pf[0:DEC, CZ:CY + PAST], Pf[0:DEC, CZ:CY + PAST], rc[0:DEC, 2:3], None,
                                      ALU.mult).then_inc(probs_ready, 1)

                def gate(g, e):
                    x = int(e[1])
                    u = use(g, e)
                    if x == 0:
                        wait(dve, zg_made, g + 1)
                    wait(dve, use_ready, u + 1)
                    dve.tensor_tensor(zg[:, x, :], zg[:, x, :], aux[u.turn(4)][:, 0:TQ], ALU.mult)\
                       .then_inc(use_free[u.turn(4)], 1)

                def take_z(g, n, j, tile):
                    wait(dve, oz_ready, g.times(GRP))
                    for m in range(2):
                        u = tile + m
                        wait(dve, used, n + 1)
                        dve.tensor_tensor(zg[:, 2 * (j // 12) + m, :], acc[u.turn(4)][:, 0:TQ], rstd_row[:, META:T],
                                          ALU.mult).then_inc(acc_free[u.turn(4)], 1)

                def low_oz(g, m):
                    wait(dve, oz_hi_made, g.times(GRP) + (m + 1))
                    dve.tensor_tensor(oz_lo[:, m, :], zg[:, m, :], oz_hi[:, m, :].bitcast(F32),
                                      ALU.subtract).then_inc(oz_ready, 1)

                def add_out(n, j, tile):
                    for m in range(2):
                        u = tile + m
                        wait(dve, used, n + 1)
                        x = xT[:, 2 * (j - 16) + m, META:T]
                        dve.tensor_tensor(x, x, acc[u.turn(4)][:, 0:TQ], ALU.add).then_inc(acc_free[u.turn(4)], 1)

                def event(g, e):
                    if e == "r":
                        q_terms(g)
                    elif e == "f":
                        q_finals(g)
                    elif e == "b":
                        q_back(g)
                    elif e[0] == "S":
                        maxima(g, e)
                    elif e[0] == "N":
                        softmax(g, e)
                    elif e[0] == "O":
                        gate(g, e)

                def chunk(g, n, j, tile):
                    low_part(dve, n + 2)
                    if 4 <= j < 8 and (g.a or g.b):
                        low_oz(g + -1, j - 4)
                    if j in (11, 15):
                        take_z(g, n, j, tile)
                    if j >= 16:
                        add_out(n, j, tile)

                for k in range(KD):
                    dve.wait_ge(xb_hi_made, k + 1)
                    dve.scalar_tensor_tensor(xb_lo[:, k, :], xT[:, k, META:T], par[:, GB0 + k:GB0 + k + 1],
                                             xb_hi[:, k, :].bitcast(F32), ALU.mult, ALU.subtract).then_inc(xb_lo_made, 1)
                dve.memset(F2[:, :].bitcast(F32), 0.0).then_inc(f_set, 1)
                own.done(dve.memset(minus[:, :], 0.0))
                own.wait()
                for buf in (qst, mx, sm):
                    own.done(dve.memset(buf[:, :, :] if buf is qst else buf[:, :], 1.0))
                own.done(dve.tensor_scalar(minus[0:BH, :], ident[0:BH, 0:BH], -1.0, None, ALU.mult))
                own.done(dve.tensor_scalar(minus[32:32 + BH, :], ident[32:32 + BH, 32:32 + BH], -1.0, None, ALU.mult))
                own.wait()
                dve.wait_ge(F_high, 1)
                dve.tensor_tensor(F2[32:32 + BH, :], F_row[:, :], F2[0:BH, :].bitcast(F32), ALU.subtract)
                turns(Count(0), True, chunk, event)
                with dve.Fori(0, GROUPS - 1) as it:
                    own.open(it, FOX_OWN)
                    turns(Count(1, 1, it), False, chunk, event)
                    own.close(GROUPS - 1)
                last = Count(GROUPS - 1)
                for e in ("O2", "N3", "O3"):
                    event(last, e)
                for m in range(GRP):
                    low_oz(last, m)
                for n, j, tile in last_steps:
                    if n.a + 2 < C_END:
                        low_part(dve, n + 2)
                    add_out(n, j, tile)
                counted["dve"] = own.n

            @block.tensor
            def _(pe):
                def free_banks(u, n):
                    for k in range(n):
                        wait(pe, use_free[(u + k).turn(4)], (u + k).rounds(4))
                    return [aux[(u + k).turn(4)] for k in range(n)]

                def q_by_token(g, tile):
                    for b in range(4):
                        wait(pe, acc_free[b], tile.rounds(4))
                    for bank, (t0, n) in zip(free_banks(use(g, "q"), 3), QT):
                        for m in range(GRP):
                            mm = pe.transpose(bank[0:n, m * P:(m + 1) * P], qf[:, m, t0:t0 + n], ident[:, :])
                        mm.then_inc(use_ready, 1)

                def q_back(g):
                    wait(pe, q_final, (g + 1).times(3))
                    banks = free_banks(use(g, "b"), 4)
                    for k, (t, m0, m1) in enumerate(BACK):
                        n = QT[t][1]
                        bank = banks[k % 4] if k < 4 else free_banks(use(g, "b", 4), 1)[0]
                        for m in range(m0, m1):
                            mm = pe.transpose(bank[:, (m - m0) * n:(m - m0 + 1) * n],
                                              q_t[0:n, t, m * P:(m + 1) * P], ident[0:n, 0:n])
                        mm.then_inc(use_ready, 1)

                def turn_keys(g, e):
                    x = int(e[1])
                    if x == 0:
                        wait(pe, kc_landed, (g + 1).times(16))
                    bank, = free_banks(use(g, e), 1)
                    for c in range(4):
                        mm = pe.transpose(bank[:, c * P:(c + 1) * P], Kc[:, c, x * P:(x + 1) * P], ident[:, :])
                    mm.then_inc(use_ready, 1)

                def scores(g, e):
                    x = int(e[1])
                    u = use(g, e)
                    if x == 0:
                        wait(pe, kt_landed, (g + 1).times(16))
                        wait(pe, sel_made, g + 1)
                        for t in range(5):
                            b = use(g, "b", t)
                            wait(pe, use_free[b.turn(4)], b.rounds(4) + 1)
                    k = use(g, f"K{x}")
                    wait(pe, use_free[k.turn(4)], k.rounds(4) + 1)
                    for part, bank in enumerate(free_banks(u, 2)):
                        todo = [(CA, WA, 0, P, kT_in[:, x, 0:WA], FP, (CA + META, tri[:, :])),
                                (CB, WB, P, P, kT_in[:, x, 0:WB], FP, (CB + META + P, tri[:, :])),
                                (CZ, WZ, 256, DEC, kT_in[:, x, 256:T], FN, (CZ, tri_new[:, :]))] if part == 0 else \
                               [(0, PAST, 256, DEC, KcT[:, :], FC, None)]
                        for c, w, t0, n, keys, f, mask_ in todo:
                            pe.matmul(bank[0:n, c:c + w], sel[:, x, 0:n], F2[:, f:f + w], start=True, stop=False)
                            if mask_:
                                m0_, m_ = mask_
                                pe.matmul(bank[0:n, m0_:m0_ + m_.shape[-1]], ident_bf[0:n, 0:n], m_, start=False,
                                          stop=False)
                            mm = pe.matmul(bank[0:n, c:c + w], qT[:, x, t0:t0 + n], keys, start=False, stop=True)
                        mm.then_inc(use_ready, 1)

                def turn_probs(g, e):
                    x = int(e[1])
                    u = use(g, e)
                    wait(pe, probs_ready, g.times(GRP) + (x + 1))
                    bank, bank2 = free_banks(u, 2)
                    for c, src in ((0, Pf[:, CA:CA + P]), (P, Pf[:, CB:CB + P]), (2 * P, Pf[:, CB + P:CB + 2 * P])):
                        pe.transpose(bank[:, c:c + P], src, ident[:, :])
                    for c in range(4):
                        mm = pe.transpose(bank[:, 3 * P + c * DEC:3 * P + (c + 1) * DEC],
                                          Pf[0:DEC, CY + c * P:CY + (c + 1) * P], ident[0:DEC, 0:DEC])
                    mm.then_inc(use_ready, 1)
                    bank = bank2
                    pe.transpose(bank[0:META, 0:P], Pf[:, CA + P:CA + WA], ident[:, :])
                    pe.transpose(bank[0:META, P:2 * P], Pf[:, CB + 2 * P:CB + WB], ident[:, :])
                    pe.transpose(bank[0:TAIL, 2 * P:2 * P + DEC], Pf[0:DEC, CZ:CZ + WZ], ident[0:DEC, 0:DEC])\
                        .then_inc(use_ready, 1)

                def outputs(g, e):
                    x = int(e[1])
                    t = use(g, f"T{x}", 1)
                    wait(pe, use_free[t.turn(4)], t.rounds(4) + 1)
                    if x == 0:
                        wait(pe, v_landed, (g + 1).times(48))
                    bank, = free_banks(use(g, e), 1)
                    d = slice(x * P, (x + 1) * P)
                    for c, w, parts in ((0, P, [(v_all[:, 0, d], PT[:, 0:P]), (v_all[0:META, 1, d], PT2[0:META, 0:P])]),
                                        (P, P, [(v_all[:, 0, d], PT[:, P:2 * P]), (v_all[:, 1, d], PT[:, 2 * P:3 * P]),
                                                (v_all[0:META, 2, d], PT2[0:META, P:2 * P])]),
                                        (2 * P, DEC, [(Vc[:, s, d], PT[:, 3 * P + s * DEC:3 * P + (s + 1) * DEC])
                                                      for s in range(4)] +
                                         [(v_all[0:TAIL, 2, d], PT2[:, 2 * P:2 * P + DEC])])):
                        for k, (v_, p_) in enumerate(parts):
                            mm = pe.matmul(bank[:, c:c + w], v_, p_, start=k == 0, stop=k == len(parts) - 1)
                    mm.then_inc(use_ready, 1)

                at_tile = {}

                def event(g, e):
                    if e == "q":
                        q_by_token(g, at_tile["now"])
                    elif e == "b":
                        q_back(g)
                    elif e[0] == "K":
                        turn_keys(g, e)
                    elif e[0] == "S":
                        scores(g, e)
                    elif e[0] == "T":
                        turn_probs(g, e)
                    elif e[0] == "O":
                        outputs(g, e)

                def chunk(g, n, j, tile):
                    if (g.a, g.b) == (0, 0) and j < 4:
                        pe.wait_ge(xb_lo_made, 4 * (j + 1))
                    at_tile["now"] = tile
                    if j < 16:
                        products(pe, n, tile, xb_hi, xb_lo, 4 * (j % 4), j % 4 == 0, j % 4 == 3)
                    else:
                        wait(pe, oz_ready, g.times(GRP))
                        products(pe, n, tile, oz_hi, oz_lo, 0, True, True)

                turns(Count(0), True, chunk, event)
                with pe.Fori(0, GROUPS - 1) as it:
                    turns(Count(1, 1, it), False, chunk, event)
                last = Count(GROUPS - 1)
                for e in ("O2", "T3", "O3"):
                    event(last, e)
                for n, j, tile in last_steps:
                    chunk(Count(GROUPS), n, j, tile)

        p5 = ExitStack()
        y_tok = sb("y_tok", [P, 3, D], F32, p5)
        p5.close()
        y_ready, y_stored = sem("y_ready"), sem("y_stored")
        y_free = [sem(f"y_free{b}") for b in range(4)]
        units = [(u, t, t0, n, c) for u, (t, t0, n, c) in enumerate(
            (t, t0, n, c) for t, (t0, n) in enumerate(QT) for c in range(4))]
        with nc.Block() as block:
            @block.tensor
            def _(pe):
                for u, t, t0, n, c in units:
                    if u >= 4:
                        pe.wait_ge(y_free[u % 4], u // 4)
                    for k in range(4):
                        mm = pe.transpose(acc[u % 4][0:n, k * P:(k + 1) * P], xT[:, 4 * c + k, META + t0:META + t0 + n],
                                          ident[:, :])
                    mm.then_inc(y_ready, 1)

            @block.vector
            def _(dve):
                for u, t, t0, n, c in units:
                    if u % 2 == 0:
                        dve.wait_ge(y_ready, u + 1)
                        dve.tensor_copy(y_tok[0:n, t, c * 512:(c + 1) * 512], acc[u % 4][0:n, :]).then_inc(y_free[u % 4], 1)

            @block.scalar
            def _(act):
                for u, t, t0, n, c in units:
                    if u % 2:
                        act.wait_ge(y_ready, u + 1)
                        act.activation(y_tok[0:n, t, c * 512:(c + 1) * 512], acc[u % 4][0:n, :], ACT.Copy)\
                           .then_inc(y_free[u % 4], 1)

            @block.sync
            def _(sp):
                for u, t, t0, n, c in units:
                    sp.wait_ge(y_free[u % 4], u // 4 + 1)
                    cut = slice(c * 512, (c + 1) * 512)
                    dst = o["y_prompt"][0, t0:t0 + n, cut] if t < 2 else o["y_sample"][0, :, cut]
                    sp.dma_start(dst, y_tok[0:n, t, cut]).then_inc(y_stored, 16)
                sp.wait_ge(y_stored, 16 * len(units))


def kernel(**inputs):
    import numpy as np
    import concourse.bacc as bacc
    from concourse.bass_utils import run_bass_kernel_spmd

    nc = bacc.Bacc("TRN2", target_bir_lowering=False, num_devices=1)
    arrays = {f"in_{name}": np.ascontiguousarray(inputs[name]) for name in INPUTS}
    ins = {name: nc.dram_tensor(f"in_{name}", arrays[f"in_{name}"].shape, F32, kind="ExternalInput").ap()
           for name in INPUTS}
    outs = {name: nc.dram_tensor(f"out_{name}", shape, F32, kind="ExternalOutput").ap() for name, shape in OUTPUTS}
    trunk(nc, ins, outs)
    got = run_bass_kernel_spmd(nc, [arrays], core_ids=[0]).results[0]
    return tuple(got[f"out_{name}"] for name, _ in OUTPUTS)


INPUTS = ["x_prompt", "x_sample", "cache_k", "cache_v", "cache_logf", "state_C", "state_n", "state_m", "state_conv",
          "meta_tokens", "a_norm_g", "a_w_in", "a_conv_w", "a_conv_b", "a_wq", "a_wk", "a_wv", "a_w_gate",
          "a_b_gate", "a_out_g", "a_skip", "a_w_out", "kv_norm_g", "w_kvf", "b_f", "k_norm_g", "b_norm_g",
          "b_w_in", "q_norm_g", "b_w_out"]
OUTPUTS = [("y_prompt", (1, SEQ, D)), ("y_sample", (1, DEC, D)),
           ("p_k", (1, TP, BH, P)), ("p_v", (1, TP, BH, P)), ("p_logf", (1, TP, BH)),
           ("p_C", (1, 1, HEADS, HD, HD)), ("p_n", (1, 1, HEADS, HD)), ("p_m", (1, 1, HEADS)),
           ("p_conv", (1, 1, PAD, INNER)),
           ("s_k", (1, DEC, BH, P)), ("s_v", (1, DEC, BH, P)), ("s_logf", (1, DEC, BH)),
           ("s_C", (1, 1, HEADS, HD, HD)), ("s_n", (1, 1, HEADS, HD)), ("s_m", (1, 1, HEADS)),
           ("s_conv", (1, 1, PAD, INNER))]
```
